# Optimizing a Trainium2 kernel written in Bass

```python
import jax, jax.numpy as jnp
from jax import lax
import numpy as np

D_MODEL = 1024
BATCH = 1
SEQ = 128
DEPTH = 1
DEC_BATCH = 1
DEC_SEQ = 512
PAST_LEN = 256

GRID_W = 64
GLA_HEADS = 4
GLA_DK = 64
GLA_DV = 128
GLA_QK = GLA_HEADS * GLA_DK
GLA_V = GLA_HEADS * GLA_DV
GLA_LOWRANK = 16
GLA_GATE_NORM = 16.0
GLA_CHUNK = 64
NA_HEADS = 8
NA_HD = 64
NA_W = NA_HEADS * NA_HD
NA_WIN_ROWS = 8
NA_WIN_COLS = 16
D_FF = 2816
CONV_W = 3
EPS = 1e-6
Q_BLOCK = 128
IN_SIZES = (GLA_QK, GLA_QK, GLA_V, GLA_V, GLA_LOWRANK, GLA_LOWRANK, NA_W, NA_W, NA_W, D_MODEL, D_MODEL)
D_IN = sum(IN_SIZES)

kernel_name = 'hybrid_gla_natten_prefix_dit_step'

def rmsnorm(x, g):
    xf = x.astype(jnp.float32)
    y = xf * lax.rsqrt(jnp.mean(xf * xf, axis=-1, keepdims=True) + EPS)
    return (y * g.astype(jnp.float32)).astype(x.dtype)

def ada_mod(cond, w, b):
    m = (jax.nn.silu(cond) @ w + b)[:, None, :]
    return jnp.split(m, 6, axis=-1)

def split_in(u):
    idx = np.cumsum(IN_SIZES)[:-1].tolist()
    return jnp.split(u, idx, axis=-1)

def gla_scan(q, k, v, log_a, s0):
    B, T, H, DK = q.shape
    DV = v.shape[-1]
    C = GLA_CHUNK
    N = T // C
    f32 = jnp.float32
    qc = q.astype(f32).reshape(B, N, C, H, DK)
    kc = k.astype(f32).reshape(B, N, C, H, DK)
    vc = v.astype(f32).reshape(B, N, C, H, DV)
    bc = jnp.cumsum(log_a.astype(f32).reshape(B, N, C, H, DK), axis=2)
    b_last = bc[:, :, -1]
    causal = jnp.tril(jnp.ones((C, C), dtype=bool))[None, None, :, :, None, None]
    diff = bc[:, :, :, None] - bc[:, :, None, :]
    decay = jnp.exp(jnp.where(causal, diff, -jnp.inf))
    scores = jnp.einsum('bnthd,bnshd,bntshd->bnhts', qc, kc, decay)
    o_intra = jnp.einsum('bnhts,bnshv->bnthv', scores, vc)
    kv_chunk = jnp.einsum('bnshd,bnshv->bnhdv', kc * jnp.exp(b_last[:, :, None] - bc), vc)

    def step(s, inp):
        a_last, kv = inp
        return jnp.exp(a_last)[..., None] * s + kv, s

    s_final, s_start = lax.scan(step, s0.astype(f32),
                                (jnp.moveaxis(b_last, 1, 0), jnp.moveaxis(kv_chunk, 1, 0)))
    o_inter = jnp.einsum('bnthd,nbhdv->bnthv', qc * jnp.exp(bc), s_start)
    o = (o_intra + o_inter).reshape(B, T, H, DV)
    return o.astype(v.dtype), s_final.astype(s0.dtype)

def gla_bidir(q, k, v, la_f, la_b, s0_f, s0_b):
    o_f, s_f = gla_scan(q, k, v, la_f, s0_f)
    flip = lambda a: jnp.flip(a, axis=1)
    o_b, s_b = gla_scan(flip(q), flip(k), flip(v), flip(la_b), s0_b)
    return o_f + flip(o_b), s_f, s_b

def ctx_attention(q, k, v):
    B, L, H, HD = q.shape
    nb = L // Q_BLOCK
    qb = jnp.moveaxis(q.reshape(B, nb, Q_BLOCK, H, HD), 1, 0)

    def one(qblk):
        s = jnp.einsum('bqhd,bkhd->bhqk', qblk, k).astype(jnp.float32) * (HD ** -0.5)
        p = jax.nn.softmax(s, axis=-1)
        return jnp.einsum('bhqk,bkhd->bqhd', p.astype(v.dtype), v)

    o = lax.map(one, qb)
    return jnp.moveaxis(o, 0, 1).reshape(B, L, H, HD)

def na_latent_attention(q, k, v, k_ctx, v_ctx, rpb):
    B, T, H, HD = q.shape
    rows = T // GRID_W
    wr = min(NA_WIN_ROWS, rows)
    wc = NA_WIN_COLS
    scale = HD ** -0.5
    qg = q.reshape(B, rows, GRID_W, H, HD)
    kg = k.reshape(B, rows, GRID_W, H, HD)
    vg = v.reshape(B, rows, GRID_W, H, HD)
    r = jnp.arange(rows)
    row_start = jnp.clip(r - wr // 2, 0, rows - wr)
    key_rows = row_start[:, None] + jnp.arange(wr)[None, :]
    k_rows = kg[:, key_rows]
    v_rows = vg[:, key_rows]
    s_loc = jnp.einsum('brqhd,brikhd->bhrqik', qg, k_rows).astype(jnp.float32) * scale
    cidx = jnp.arange(GRID_W)
    col_start = jnp.clip(cidx - wc // 2, 0, GRID_W - wc)
    in_win = (cidx[None, :] >= col_start[:, None]) & (cidx[None, :] < col_start[:, None] + wc)
    dr_idx = key_rows - r[:, None] + NA_WIN_ROWS - 1
    dc_idx = jnp.clip(cidx[None, :] - cidx[:, None], -(wc - 1), wc - 1) + NA_WIN_COLS - 1
    bias = rpb.astype(jnp.float32)[:, dr_idx[:, None, :, None], dc_idx[None, :, None, :]]
    s_loc = jnp.where(in_win[None, None, None, :, None, :], s_loc + bias[None], -jnp.inf)
    n_loc = wr * GRID_W
    s_ctx = jnp.einsum('brqhd,blhd->bhrql', qg, k_ctx).astype(jnp.float32) * scale
    s = jnp.concatenate([s_loc.reshape(B, H, rows, GRID_W, n_loc), s_ctx], axis=-1)
    p = jax.nn.softmax(s, axis=-1).astype(v.dtype)
    p_loc = p[..., :n_loc].reshape(B, H, rows, GRID_W, wr, GRID_W)
    p_ctx = p[..., n_loc:]
    o = (jnp.einsum('bhrqik,brikhd->brqhd', p_loc, v_rows)
         + jnp.einsum('bhrql,blhd->brqhd', p_ctx, v_ctx))
    return o.reshape(B, T, H, HD)

def conv_ffn(h, w_up, w_conv, b_conv, w_down):
    u = h @ w_up
    ch = u.shape[-1]
    u = lax.conv_general_dilated(u, w_conv[:, None, :], window_strides=(1,),
                                 padding=((CONV_W // 2, CONV_W // 2),),
                                 dimension_numbers=('NWC', 'WIO', 'NWC'),
                                 feature_group_count=ch) + b_conv
    a, g = jnp.split(u, 2, axis=-1)
    return (a * jax.nn.silu(g)) @ w_down

def block(x, cond, lp, ctx=None):
    (w_ada, b_ada, g_mix, w_in, w_af, b_af, w_ab, b_ab, g_gla, g_qn, g_kn, rpb,
     w_gla_o, w_na_o, w_out, g_ffn, w_up, w_conv, b_conv, w_down) = lp
    B, T, _ = x.shape
    sh1, sc1, gt1, sh2, sc2, gt2 = ada_mod(cond, w_ada, b_ada)
    h = rmsnorm(x, g_mix) * (1 + sc1) + sh1
    gq, gk, gv, gr, zf, zb, nq, nk, nv, m_gla, m_na = split_in(h @ w_in)
    q = gq.reshape(B, T, GLA_HEADS, GLA_DK) * (GLA_DK ** -0.5)
    k = gk.reshape(B, T, GLA_HEADS, GLA_DK)
    v = gv.reshape(B, T, GLA_HEADS, GLA_DV)
    la_f = (jax.nn.log_sigmoid((zf @ w_af + b_af).astype(jnp.float32)) / GLA_GATE_NORM).reshape(B, T, GLA_HEADS, GLA_DK)
    la_b = (jax.nn.log_sigmoid((zb @ w_ab + b_ab).astype(jnp.float32)) / GLA_GATE_NORM).reshape(B, T, GLA_HEADS, GLA_DK)
    if ctx is None:
        s0_f = jnp.zeros((B, GLA_HEADS, GLA_DK, GLA_DV), x.dtype)
        s0_b = s0_f
    else:
        k_ctx, v_ctx, s0_f, s0_b = ctx
    o_gla, s_f, s_b = gla_bidir(q, k, v, la_f, la_b, s0_f, s0_b)
    b_gla = (rmsnorm(o_gla, g_gla).reshape(B, T, GLA_V) * jax.nn.silu(gr)) @ w_gla_o
    qn = rmsnorm(nq.reshape(B, T, NA_HEADS, NA_HD), g_qn)
    kn = rmsnorm(nk.reshape(B, T, NA_HEADS, NA_HD), g_kn)
    vn = nv.reshape(B, T, NA_HEADS, NA_HD)
    if ctx is None:
        o_na = ctx_attention(qn, kn, vn)
    else:
        o_na = na_latent_attention(qn, kn, vn, k_ctx, v_ctx, rpb)
    b_na = o_na.reshape(B, T, NA_W) @ w_na_o
    mix = (jax.nn.sigmoid(m_gla) * b_gla + jax.nn.sigmoid(m_na) * b_na) @ w_out
    x = x + gt1 * mix
    h2 = rmsnorm(x, g_ffn) * (1 + sc2) + sh2
    x = x + gt2 * conv_ffn(h2, w_up, w_conv, b_conv, w_down)
    return x, (kn, vn, s_f, s_b)

def setup_inputs(seed: int = 0) -> dict:
    key = jax.random.key(seed)
    ks = jax.random.split(key, 28)
    nrm = lambda kk, shape, s=1.0: jax.random.normal(kk, shape, jnp.float32) * s
    gain = lambda kk, shape: 1.0 + 0.02 * jax.random.normal(kk, shape, jnp.float32)
    L = DEPTH
    return {
        'x_prompt': nrm(ks[0], (BATCH, SEQ, D_MODEL)),
        'x_sample': nrm(ks[1], (DEC_BATCH, DEC_SEQ, D_MODEL)),
        'c': nrm(ks[2], (DEC_BATCH, D_MODEL)),
        'cache_na_k': nrm(ks[3], (DEC_BATCH, L, PAST_LEN, NA_HEADS, NA_HD)),
        'cache_na_v': nrm(ks[4], (DEC_BATCH, L, PAST_LEN, NA_HEADS, NA_HD)),
        'state_gla_fwd': nrm(ks[5], (DEC_BATCH, L, GLA_HEADS, GLA_DK, GLA_DV), 2.0),
        'state_gla_bwd': nrm(ks[6], (DEC_BATCH, L, GLA_HEADS, GLA_DK, GLA_DV), 2.0),
        'c_ctx': nrm(ks[7], (D_MODEL,)),
        'w_ada': nrm(ks[8], (L, D_MODEL, 6 * D_MODEL), 0.3 * D_MODEL ** -0.5),
        'b_ada': nrm(ks[9], (L, 6 * D_MODEL), 0.02),
        'g_norm_mix': gain(ks[10], (L, D_MODEL)),
        'w_in': nrm(ks[11], (L, D_MODEL, D_IN), D_MODEL ** -0.5),
        'w_alpha_fwd': nrm(ks[12], (L, GLA_LOWRANK, GLA_QK), GLA_LOWRANK ** -0.5),
        'b_alpha_fwd': nrm(ks[13], (L, GLA_QK), 0.1),
        'w_alpha_bwd': nrm(ks[14], (L, GLA_LOWRANK, GLA_QK), GLA_LOWRANK ** -0.5),
        'b_alpha_bwd': nrm(ks[15], (L, GLA_QK), 0.1),
        'g_gla_norm': gain(ks[16], (L, GLA_DV)),
        'g_q_norm': gain(ks[17], (L, NA_HD)),
        'g_k_norm': gain(ks[18], (L, NA_HD)),
        'rpb': nrm(ks[19], (L, NA_HEADS, 2 * NA_WIN_ROWS - 1, 2 * NA_WIN_COLS - 1), 0.1),
        'w_gla_o': nrm(ks[20], (L, GLA_V, D_MODEL), GLA_V ** -0.5),
        'w_na_o': nrm(ks[21], (L, NA_W, D_MODEL), NA_W ** -0.5),
        'w_out': nrm(ks[22], (L, D_MODEL, D_MODEL), D_MODEL ** -0.5),
        'g_norm_ffn': gain(ks[23], (L, D_MODEL)),
        'w_up': nrm(ks[24], (L, D_MODEL, 2 * D_FF), D_MODEL ** -0.5),
        'w_conv': nrm(ks[25], (L, CONV_W, 2 * D_FF), CONV_W ** -0.5),
        'b_conv': nrm(ks[26], (L, 2 * D_FF), 0.02),
        'w_down': nrm(ks[27], (L, D_FF, D_MODEL), D_FF ** -0.5),
    }

def reference(x_prompt, x_sample, c, cache_na_k, cache_na_v, state_gla_fwd, state_gla_bwd,
              c_ctx, w_ada, b_ada, g_norm_mix, w_in, w_alpha_fwd, b_alpha_fwd, w_alpha_bwd,
              b_alpha_bwd, g_gla_norm, g_q_norm, g_k_norm, rpb, w_gla_o, w_na_o, w_out,
              g_norm_ffn, w_up, w_conv, b_conv, w_down):
    xp = x_prompt
    xs = x_sample
    cond_ctx = c_ctx[None, :]
    new_k, new_v, new_sf, new_sb = [], [], [], []
    for l in range(DEPTH):
        lp = (w_ada[l], b_ada[l], g_norm_mix[l], w_in[l], w_alpha_fwd[l], b_alpha_fwd[l],
              w_alpha_bwd[l], b_alpha_bwd[l], g_gla_norm[l], g_q_norm[l], g_k_norm[l], rpb[l],
              w_gla_o[l], w_na_o[l], w_out[l], g_norm_ffn[l], w_up[l], w_conv[l], b_conv[l], w_down[l])
        xp, (kc, vc, sf, sb) = block(xp, cond_ctx, lp)
        new_k.append(kc)
        new_v.append(vc)
        new_sf.append(sf)
        new_sb.append(sb)
        xs, _ = block(xs, c, lp, (cache_na_k[:, l], cache_na_v[:, l], state_gla_fwd[:, l], state_gla_bwd[:, l]))
    new_cache_na_k = jnp.stack(new_k, axis=1)
    new_cache_na_v = jnp.stack(new_v, axis=1)
    new_state_gla_fwd = jnp.stack(new_sf, axis=1)
    new_state_gla_bwd = jnp.stack(new_sb, axis=1)
    return (xp, xs, new_cache_na_k, new_cache_na_v, new_state_gla_fwd, new_state_gla_bwd)


_drawn_inputs = setup_inputs


def setup_inputs(seed=0):
    import zlib

    import numpy as np

    out = dict(_drawn_inputs(seed))
    spreads = {}
    factors = {'cache_na_k': 8.0,
     'cache_na_v': 7.984,
     'state_gla_fwd': 8.0,
     'state_gla_bwd': 8.0,
     'g_gla_norm': 37.787,
     'g_q_norm': 8.0,
     'g_k_norm': 8.049,
     'rpb': 8.0,
     'w_na_o': 2.776,
     'g_norm_ffn': 8.0,
     'b_conv': 8.0}
    for name, (base, spread) in spreads.items():
        noise = np.random.default_rng([zlib.crc32(name.encode()), seed]).standard_normal(out[name].shape)
        drawn = base * np.exp(spread * noise) if base else spread * noise
        out[name] = __import__('jax').numpy.asarray(drawn.astype(out[name].dtype))
    for name, factor in factors.items():
        out[name] = (out[name] * factor).astype(out[name].dtype)
    return out
```

```python
from contextlib import ExitStack

import concourse.bass as bass
from concourse import mybir

P = 128
F32 = mybir.dt.float32
F32R = mybir.dt.float32r
U8 = mybir.dt.uint8
I32 = mybir.dt.int32
ACT = mybir.ActivationFunctionType
ALU = mybir.AluOpType
AX = mybir.AxisListType

D = 1024
NK = D // P
SAMPLE, CONTEXT = 512, 128
TOK = SAMPLE + CONTEXT
NT = TOK // P
HALF = TOK // 2
BANK = 512
PAST = 256
GH, DK, DV = 4, 64, 128
NH, HD = 8, 64
GRID_W, ROWS = 64, 8
GC = 16
WR, WC = 8, 16
D_FF = 2816
NF = D_FF // P
EPS = 1e-6
MASKED = -8e30
IN_Z = 1536
IN_NA, IN_MGLA, IN_MNA = 1568, 3104, 4128

C_Z = 0
C_GLA = 1
C_NA = C_GLA + 12
C_MG = C_NA + 12
C_POST = C_MG + 8
C_OUT = C_POST + 16
C_UP = C_OUT + 8
C_DOWN = C_UP + 2 * NF
DOWN_K = [8, 7, 7]

ADA_FIRST = 16
ADA_SLOTS = 6
ADA_HI = 4
ADA_LAG = 2
ADA_REST = 48 - ADA_FIRST

V_W0, V_BADA, V_GMIX, V_GFFN, V_BAF, V_BAB, V_GGLA, V_GQ, V_GK = 0, 44, 92, 100, 108, 110, 112, 113, 114
V_W1, V_W2, V_C, V_CCTX = 0, 44, 88, 96
ROWS_0, ROWS_1, ROWS_2 = 115, 104, 44

KEYS = [(0, 2, 384), (0, 3, 0), (1, 3, 0), (2, 2, 640)]
N_LEVEL = 8


def hybrid_dit_step(nc, x_prompt, x_sample, c, cache_k, cache_v, state_f, state_b, c_ctx, w_ada, b_ada,
                    g_mix, w_in, w_af, b_af, w_ab, b_ab, g_gla, g_q, g_k, rpb, w_gla_o, w_na_o, w_out,
                    g_ffn, w_up, w_conv, b_conv, w_down, tables, level_masks,
                    y_prompt, y_sample, new_k, new_v, new_sf, new_sb):
    with ExitStack() as ctx:
        base = 16512

        def at(name, offset, shape, dt=F32):
            return nc.alloc_sbuf_tensor_at(name, [P] + list(shape), dt, offset=base + offset)

        def sem(name):
            return ctx.enter_context(nc.semaphore(name))

        ident = at("ident", 0, [P])
        ones = at("ones", 512, [P])
        blk64 = at("blk64", 1024, [P])
        vec = at("vec", 1536, [3, P])
        mod = at("mod", 3072, [48, 2])
        a1 = at("a1", 3456, [NK, 2])
        a2 = at("a2", 3456, [NK, 2])
        cond4 = at("cond4", 3520, [NK, 4], F32R)
        eps = at("eps", 3648, [1])
        one = at("one", 3680, [1])
        pick = vec[:, 2, ROWS_2:ROWS_2 + 2]
        RAW = 3712
        wraw = at("wraw", RAW, [2, 8, P])
        whi = at("whi", RAW + 8192, [2, 8, P], F32R)
        wlo = at("wlo", RAW + 16384, [2, 8, P], F32R)
        H = RAW + 24576
        h_hi = at("h_hi", H, [NK, TOK], F32R)
        h_lo = at("h_lo", H + 20480, [NK, TOK], F32R)
        R = H + 40960
        x_rows = at("x_rows", R + 25600, [NT, D])
        ada_first = at("ada_first", R + 46080, [ADA_SLOTS, 2, 4 * P])
        ada_lo = at("ada_lo", R + 46080, [ADA_SLOTS, 2, 4 * P], F32R)
        ada_hi = at("ada_hi", H, [ADA_HI, 2, 4 * P], F32R)
        mod_rows = at("mod_rows", H + 20480, [4, 4 * P])
        xT = at("xT", R + 107616, [NK, TOK])
        x_sq = at("x_sq", R + 87136, [2, TOK])
        rstd = at("rstd", R + 92256, [TOK])
        h_t = at("h_t", R + 94816, [TOK])
        h_f = at("h_f", R + 97376, [2, TOK])
        cond_sig = at("cond_sig", R + 102496, [2 * NK])
        cond = at("cond", R + 102560, [2, NK])
        rpb_rows = at("rpb_rows", R + 0, [NH, ROWS, 31])
        rpb_wide = at("rpb_wide", R + 128096, [NH, ROWS, 48])
        vec_rows = at("vec_rows", R + 104000, [3, P])
        kc_tok = at("kc_tok", R + 76800, [2, NH * HD])
        window = at("window", R + 0, [896])
        level_mask = at("level_mask", R + 3584, [N_LEVEL, P], U8)
        bias8 = at("bias8", R + 5120, [NH, 384])
        kcT = at("kcT", R + 17408, [4, PAST])
        vc = at("vc", R + 21504, [2, NH * HD])
        nqk = at("nqk", R + 25600, [8, TOK])
        nv_tok = at("nv_tok", R + 46080, [NT, NH * HD])
        v_tok = at("v_tok", R + 56320, [NT, GH * DV])
        lvl = at("lvl", R + 66560, [2, 4, TOK])
        la_e = at("la_e", R + 66560, [4, TOK])
        la_m = at("la_m", R + 76800, [4, TOK])
        Y = at("Y", R + 87040, [4, NT, P + 1])
        U = at("U", R + 97376, [12, TOK])
        A = at("A", R + 107616, [2, NT, 2, P])
        kt = at("kt", R + 97376, [2, NT, 256])
        S = at("S", R + 87040, [2, 4, 2, DV])
        nvraw = at("nvraw", R + 128096, [4, TOK])
        oT = at("oT", R + 128096, [GH, TOK])
        z = at("z", R + 138336, [TOK])
        w_alpha = at("w_alpha", R + 140896, [4 * P])
        decay = at("decay", R + 138336, [4, NT])
        s_out = at("s_out", R + 140896, [2, 2, DV])
        og_sq = at("og_sq", R + 97376, [2, TOK])
        og_rs = at("og_rs", R + 102496, [2, TOK])
        og_hi = at("og_hi", R + 66560, [GH, TOK], F32R)
        og_lo = at("og_lo", R + 76800, [GH, TOK], F32R)
        sg = at("sg", R + 107616, [NK, TOK])
        o_tok = at("o_tok", R + 128096, [NT, NH * HD])
        qk_rs = at("qk_rs", R + 56320, [2, TOK])
        qk_n = at("qk_n", R + 61440, [2, TOK])
        kc_pair = at("kc_pair", R + 87040, [PAST])
        bias = at("bias", R + 88064, [2, 896])
        sc = at("sc", R + 95232, [2, TOK])
        pT = at("pT", R + 100352, [2, TOK])
        k_out = at("k_out", R + 105472, [P])
        mx = at("mx", R + 105984, [2, 10])
        nmx = at("nmx", R + 106080, [10])
        psm = at("psm", R + 106144, [10])
        rin = at("rin", R + 106208, [10])
        ona_hi = at("ona_hi", R + 87040, [4, TOK], F32R)
        ona_lo = at("ona_lo", R + 97280, [4, TOK], F32R)
        mix_hi = at("mix_hi", R + 0, [NK, TOK], F32R)
        mix_lo = at("mix_lo", R + 20480, [NK, TOK], F32R)
        ada_rest = at("ada_rest", R + 40960, [4, 2, 4 * P])
        ada_rest_lo = at("ada_rest_lo", R + 40960, [4, 2, 4 * P], F32R)
        ada_rest_hi = at("ada_rest_hi", R + 128096, [2, 2, 4 * P], F32R)
        rest_rows = at("rest_rows", R + 136288, [4 * P])
        sn = at("sn", R + 57344, [TOK])
        t1 = at("t1", R + 59904, [TOK])
        t2 = at("t2", R + 62464, [TOK])
        x_cols = at("x_cols", R + 57344, [2, NT, P])
        x2_sq = at("x2_sq", R + 62464, [2, TOK])
        zeros = at("zeros", R + 67584, [HALF])
        x2 = at("x2", R + 123008, [NK, TOK])
        rstd2 = at("rstd2", R + 0, [TOK])
        h2_t = at("h2_t", R + 2560, [TOK])
        h2_f = at("h2_f", R + 5120, [2, TOK])
        ua = at("ua", R + 0, [TOK + 3])
        ug = at("ug", R + 2592, [TOK + 3])
        ca = at("ca", R + 5184, [TOK + 1])
        cg = at("cg", R + 7776, [TOK + 1])
        act_hi = at("act_hi", R + 10368, [NF, TOK], F32R)
        act_lo = at("act_lo", R + 66688, [NF, TOK], F32R)
        yT = at("yT", R + 0, [2, TOK])
        y_tok = at("y_tok", R + 5120, [2, NT, P])

        PJ = ctx.enter_context(nc.psum_tensor("PJ", [P, 4 * BANK], F32))
        PA = ctx.enter_context(nc.psum_tensor("PA", [P, 4 * BANK], F32))

        def halves(ps, pair):
            return ps[:, pair * 2 * BANK:(pair + 1) * 2 * BANK].rearrange("p (b n) -> p b n", b=2)[:, :, 0:HALF]

        def by_half(t):
            return t.rearrange("p (b n) -> p b n", b=2)

        tab_in = sem("tab_in")
        ones_in, x_in = sem("ones_in"), sem("x_in")
        cvec_in, vec_in = sem("cvec_in"), sem("vec_in")
        past_in, mask_in = sem("past_in"), sem("mask_in")
        rpb_in, rpb_moved = sem("rpb_in"), sem("rpb_moved")
        ada_in = [sem(f"ada_in{i}") for i in range(ADA_SLOTS)]
        ada_hid, ada_lod, ada_used = sem("ada_hid"), sem("ada_lod"), sem("ada_used")
        raw_in = [sem("raw_in0"), sem("raw_in1")]
        hi_done, lo_done, slot_freed = sem("hi_done"), sem("lo_done"), sem("slot_freed")
        const_set = sem("const_set")
        vec_ps, vec_done = sem("vec_ps"), sem("vec_done")
        cond_sg, cond_done, cvec_done = sem("cond_sg"), sem("cond_done"), sem("cvec_done")
        xt_ps, xt_cp, xt_sq, xt_st = sem("xt_ps"), sem("xt_cp"), sem("xt_sq"), sem("xt_st")
        kct_ps, kct_cp = sem("kct_ps"), sem("kct_cp")
        rows_set, mod_ps, mod_set, a1_set = sem("rows_set"), sem("mod_ps"), sem("mod_set"), sem("a1_set")
        rs_ln, rs_done = sem("rs_ln"), sem("rs_done")
        ht_set, hf_set, hhi_set, hlo_set = sem("ht_set"), sem("hf_set"), sem("hhi_set"), sem("hlo_set")
        bias8_set = sem("bias8_set")
        tile_ready, tile_freed = sem("tile_ready"), sem("tile_freed")
        la_ps, la_abs, la_exp, la_ln, la_min, la_sub, la_sum = (sem(n) for n in (
            "la_ps", "la_abs", "la_exp", "la_ln", "la_min", "la_sub", "la_sum"))
        q_scaled = sem("q_scaled")
        vt_ps = sem("vt_ps")
        lv_arg, lv_exp, lv_set, lv_ps, lv_cp = (sem(n) for n in (
            "lv_arg", "lv_exp", "lv_set", "lv_ps", "lv_cp"))
        kt_ps = sem("kt_ps")
        decay_set, s0_in, kv_ps, s_set, s_copied, s_stored = (sem(n) for n in (
            "decay_set", "s0_in", "kv_ps", "s_set", "s_copied", "s_stored"))
        gr_silu, o_ps, o_cp = sem("gr_silu"), sem("o_ps"), sem("o_cp")
        og_sqd, og_st, og_ln, og_rsd, og_n, og_g, og_hid, og_lod = (sem(n) for n in (
            "og_sqd", "og_st", "og_ln", "og_rsd", "og_n", "og_g", "og_hid", "og_lod"))
        nvt_ps, nvt_cp, nv_stored = sem("nvt_ps"), sem("nvt_cp"), sem("nv_stored")
        bias_set, sq_set, sq_ps, sq_ln, sq_rs, qk_set, kcp_set, ko_ps, ko_cp, ko_stored = (sem(n) for n in (
            "bias_set", "sq_set", "sq_ps", "sq_ln", "sq_rs", "qk_set", "kcp_set", "ko_ps", "ko_cp", "ko_stored"))
        sc_ps, sc_mx, sc_cp, sc_exp, pt_ps, pt_cp, pv_ps, rin_set, pv_cp, gate_cp = (sem(n) for n in (
            "sc_ps", "sc_mx", "sc_cp", "sc_exp", "pt_ps", "pt_cp", "pv_ps", "rin_set", "pv_cp", "gate_cp"))
        on_ps, on_hi, on_lo = sem("on_ps"), sem("on_hi"), sem("on_lo")
        mna_ps, bg_ps, bn_ps, sn_set, t1_set, t2_set, mixf_set, mixhi_set, mixlo_set = (sem(n) for n in (
            "mna_ps", "bg_ps", "bn_ps", "sn_set", "t1_set", "t2_set", "mixf_set", "mixhi_set", "mixlo_set"))
        ada2_in = [sem(f"ada2_in{i}") for i in range(4)]
        ada2_hid, ada2_lod, ada2_used, ada2_rows, ada2_ps, ada2_cp, mod_all = (sem(n) for n in (
            "ada2_hid", "ada2_lod", "ada2_used", "ada2_rows", "ada2_ps", "ada2_cp", "mod_all"))
        xc_in = [sem("xc_in0"), sem("xc_in1")]
        out_ps, xc_ps, xc_cp, x2_set, x2_sqd, x2_st, zero_set = (sem(n) for n in (
            "out_ps", "xc_ps", "xc_cp", "x2_set", "x2_sqd", "x2_st", "zero_set"))
        rs2_ln, rs2_done, h2t_set, h2f_set, h2hi_set, h2lo_set, pad_set = (sem(n) for n in (
            "rs2_ln", "rs2_done", "h2t_set", "h2f_set", "h2hi_set", "h2lo_set", "pad_set"))
        up_ps, ua_set, ug_set, ca_step, cg_step, silu_set, prod_set, acthi_set, actlo_set = (sem(n) for n in (
            "up_ps", "ua_set", "ug_set", "ca_step", "cg_step", "silu_set", "prod_set", "acthi_set", "actlo_set"))
        dn_ps, y_set, yt_ps, y_cp, y_stored = (sem(n) for n in ("dn_ps", "y_set", "yt_ps", "y_cp", "y_stored"))

        w_in_v = w_in[0].rearrange("(k p) n -> p k n", p=P)
        w_ada_v = w_ada[0].rearrange("(k p) n -> p k n", p=P)
        w_go_v = w_gla_o[0].rearrange("(k p) n -> p k n", p=P)
        w_no_v = w_na_o[0].rearrange("(k p) n -> p k n", p=P)
        w_out_v = w_out[0].rearrange("(k p) n -> p k n", p=P)
        w_up_v = w_up[0].rearrange("(k p) n -> p k n", p=P)
        w_dn_v = w_down[0].rearrange("(k p) n -> p k n", p=P)
        xs_v = x_sample[0].rearrange("(t p) d -> p t d", p=P)
        ys_v = y_sample[0].rearrange("(t p) d -> p t d", p=P)

        block = ctx.enter_context(nc.Block())

        @block.sync
        def _(sp):
            def chunk(slot, n, src, col, free, k=8, src2=None):
                if free is not None:
                    sp.wait_ge(lo_done, free)
                    sp.sem_inc(slot_freed, 1)
                if src2 is None:
                    sp.dma_start(wraw[:, slot, 0:4, :], src[:, n:n + 4, bass.ds(col, P)]).then_inc(raw_in[slot], 16)
                    sp.dma_start(wraw[:, slot, 4:k, :], src[:, n + 4:n + k, bass.ds(col, P)]).then_inc(raw_in[slot], 16)
                else:
                    sp.dma_start(wraw[:, slot, 0:4, :], src[:, 0:4, bass.ds(col, P)]).then_inc(raw_in[slot], 16)
                    sp.dma_start(wraw[:, slot, 4:8, :], src2[:, 0:4, bass.ds(col, P)]).then_inc(raw_in[slot], 16)

            def ada_piece(at_, q):
                return w_ada_v[:, 2 * q:2 * q + 2, at_:at_ + 4 * P] if isinstance(at_, int) else \
                    w_ada_v[:, 2 * q:2 * q + 2, bass.ds(at_, 4 * P)]

            sp.dma_start(ident[:, :], tables[:, 0:128]).then_inc(tab_in, 16)
            sp.dma_start(x_rows[:, 0:NT - 1, :], xs_v).then_inc(x_in, 16)
            sp.dma_start(x_rows[:, NT - 1, :], x_prompt[0]).then_inc(x_in, 16)
            sp.dma_start(ones[:, :], tables[:, 128:256]).then_inc(ones_in, 16)
            sp.dma_start(blk64[:, :], tables[:, 256:384]).then_inc(ones_in, 16)
            for a in range(ADA_FIRST):
                if a >= ADA_SLOTS:
                    sp.wait_ge(ada_used, a - ADA_SLOTS + 1)
                sp.dma_start(ada_first[:, a % ADA_SLOTS, :, :], ada_piece(a // 4 * 4 * P, a % 4))\
                  .then_inc(ada_in[a % ADA_SLOTS], 16)
            chunk(0, 0, w_in_v, IN_Z, None)
            with sp.Fori(0, 6) as i:
                chunk(1, 0, w_in_v, i * 256, i * 2)
                chunk(0, 0, w_in_v, i * 256 + 128, i * 2 + 1)
            with sp.Fori(0, 10) as i:
                chunk(1, 0, w_in_v, i * 256 + IN_NA, i * 2 + C_NA - 1)
                chunk(0, 0, w_in_v, i * 256 + (IN_NA + 128), i * 2 + C_NA)
            chunk(1, 0, w_in_v, IN_MNA, C_POST - 1)
            chunk(0, 0, w_go_v, 0, C_POST, src2=w_no_v)
            sp.wait_ge(nvt_cp, NT)
            sp.wait_ge(pv_cp, 40)
            sp.wait_ge(nv_stored, 16)

            def ada_rest_piece(a, at_):
                sp.dma_start(ada_rest[:, a, :, :], ada_piece(at_, a)).then_inc(ada2_in[a], 16)

            for a in range(4):
                ada_rest_piece(a, ADA_FIRST * P)
            with sp.Fori(0, NK - 1) as j:
                chunk(1, 0, w_in_v, j * 128 + (IN_MNA + P), j * 2 + (C_POST + 1))
                sp.wait_ge(ada2_used, j * 4 + 2)
                sp.sem_inc(slot_freed, 1)
                for a in (0, 1):
                    ada_rest_piece(a, j * 512 + (ADA_FIRST + 4) * P)
                chunk(0, 0, w_go_v, j * 128 + P, j * 2 + (C_POST + 2), src2=w_no_v)
                sp.wait_ge(ada2_used, j * 4 + 4)
                sp.sem_inc(slot_freed, 1)
                for a in (2, 3):
                    ada_rest_piece(a, j * 512 + (ADA_FIRST + 4) * P)
            with sp.Fori(0, 4) as i:
                for b in range(2):
                    chunk((b + 1) % 2, 0, w_out_v, i * 256 + b * 128, i * 2 + (C_OUT - 1 + b))
                sp.wait_ge(mixlo_set, NK)
                sp.wait_ge(xc_ps, i * 2)
                sp.sem_inc(slot_freed, 1)
                for b in range(2):
                    sp.dma_start(x_cols[:, b, 0:4, :], xs_v[:, :, bass.ds(i * 256 + b * 128, P)]).then_inc(xc_in[b], 16)
                    sp.dma_start(x_cols[:, b, 4, :], x_prompt[0][:, bass.ds(i * 256 + b * 128, P)]).then_inc(xc_in[b], 16)
            with sp.Fori(0, NF) as j:
                chunk(1, 0, w_up_v, j * 128, j * 2 + C_UP - 1)
                chunk(0, 0, w_up_v, j * 128 + D_FF, j * 2 + C_UP)
            with sp.Fori(0, 4) as i:
                for b in range(2):
                    for q in range(3):
                        n = 3 * b + q
                        chunk((n + 1) % 2, sum(DOWN_K[:q]), w_dn_v, i * 256 + b * 128, i * 6 + (C_DOWN - 1 + n), k=DOWN_K[q])

        @block.gpsimd
        def _(pool):
            def lo(slot, ready, k=8):
                pool.wait_ge(hi_done, ready)
                pool.tensor_tensor(wlo[:, slot, 0:k, :], wraw[:, slot, 0:k, :],
                                   whi[:, slot, 0:k, :].bitcast(F32), ALU.subtract).then_inc(lo_done, 1)

            pool.dma_start(kc_tok[:, :, :], cache_k[0, 0].rearrange("(b p) h d -> p b (h d)", p=P)).then_inc(past_in, 16)
            pool.dma_start(vc[:, :, :], cache_v[0, 0].rearrange("(b p) h d -> p b (h d)", p=P)).then_inc(past_in, 16)
            for q in range(ROWS):
                src = rpb[0, :, ROWS - 1 - q:2 * ROWS - 1 - q, :].unsqueeze(0).to_broadcast([GC, NH, ROWS, 31])
                pool.dma_start(rpb_rows[q * GC:(q + 1) * GC, :, :, :], src).then_inc(rpb_in, 16)
            pool.wait_ge(const_set, 4)
            pool.dma_start(w_alpha[0:16, 0:256], w_af[0]).then_inc(past_in, 16)
            pool.dma_start(w_alpha[16:32, 256:512], w_ab[0]).then_inc(past_in, 16)
            pool.wait_ge(rpb_in, 16 * ROWS)
            for q in range(GC):
                pool.dma_start(rpb_wide[q:q + 7 * GC + 1:GC, :, :, q + 1:q + 32], rpb_rows[q:q + 7 * GC + 1:GC, :, :, :])\
                    .then_inc(rpb_moved, 16)
            pool.wait_ge(rpb_moved, 16 * GC)
            for o in range(3):
                ins = pool.tensor_scalar(bias8[:, :, o * P:(o + 1) * P].rearrange("p h (r c) -> p h r c", c=GC),
                                         rpb_wide[:, :, :, o * GC:(o + 1) * GC], 8.0, None, ALU.mult)
            ins.then_inc(bias8_set, 1)
            lo(0, 1)
            with pool.Fori(0, 6) as i:
                lo(1, i * 2 + C_GLA + 1)
                lo(0, i * 2 + C_GLA + 2)
            with pool.Fori(0, 6) as i:
                lo(1, i * 2 + C_NA + 1)
                lo(0, i * 2 + C_NA + 2)
            pool.wait_ge(bias8_set, 1)
            pool.wait_ge(mask_in, 32)
            pool.wait_ge(o_ps, 6)
            with pool.Fori(0, 4) as j:
                pool.wait_ge(sc_cp, j * 10)
                b8 = bias8[:, bass.ds(j * 2, 2), :]
                for lo_at, n, src in ((0, 384, 0), (384, 256, 128), (640, 256, 0)):
                    mk = window[:, lo_at:lo_at + n].unsqueeze(1).to_broadcast([P, 2, n])
                    pool.tensor_tensor(bias[:, :, lo_at:lo_at + n], b8[:, :, src:src + n], mk, ALU.add)\
                        .then_inc(bias_set, 1)
                lo(1, j * 2 + C_MG + 1)
                lo(0, j * 2 + C_MG + 2)
            with pool.Fori(0, NK) as j:
                lo(1, j * 2 + C_POST + 1)
                lo(0, j * 2 + C_POST + 2)
            with pool.Fori(0, 4) as j:
                lo(1, j * 2 + C_OUT + 1)
                lo(0, j * 2 + C_OUT + 2)
            with pool.Fori(0, NF) as j:
                lo(1, j * 2 + C_UP + 1)
                lo(0, j * 2 + C_UP + 2)
            with pool.Fori(0, 4) as i:
                for n in range(6):
                    lo((n + 1) % 2, i * 6 + C_DOWN + 1 + n)

        @block.tensor
        def _(pe):
            def project(slot, ready, hi, lo, ps, pair, k0=0, k1=8, w0=0, start=True, stop=True, done=None):
                if ready is not None:
                    pe.wait_ge(lo_done, ready)
                for k in range(k0, k1):
                    for b in range(2):
                        out = ps[:, (2 * pair + b) * BANK:(2 * pair + b) * BANK + HALF]
                        tok = slice(b * HALF, (b + 1) * HALF)
                        pe.matmul(out, whi[:, slot, w0 + k, :], hi(k)[:, tok], start=start and k == k0, stop=False)
                        pe.matmul(out, whi[:, slot, w0 + k, :], lo(k)[:, tok], start=False, stop=False)
                    for b in range(2):
                        out = ps[:, (2 * pair + b) * BANK:(2 * pair + b) * BANK + HALF]
                        tok = slice(b * HALF, (b + 1) * HALF)
                        mm = pe.matmul(out, wlo[:, slot, w0 + k, :], hi(k)[:, tok], start=False, stop=stop and k == k1 - 1)
                if done is not None:
                    mm.then_inc(done, 1)

            hh = lambda k: h_hi[:, k, :]
            hl = lambda k: h_lo[:, k, :]

            pe.wait_ge(tab_in, 32)
            pe.wait_ge(cvec_in, 16 * 3)
            pe.transpose(PA[:, 1024:1024 + ROWS_1], vec_rows[0:ROWS_1, 1, :], ident[0:ROWS_1, 0:ROWS_1]).then_inc(vec_ps, 1)
            pe.wait_ge(x_in, 32)
            pe.wait_ge(ones_in, 32)

            def x_stats(f):
                pe.wait_ge(xt_sq, f + 1)
                for b in range(2):
                    mm = pe.matmul(PJ[:, b * BANK:b * BANK + HALF], ones[:, :], x_sq[:, f % 2, b * HALF:(b + 1) * HALF],
                                   start=f == 0, stop=f == NK - 1)
                mm.then_inc(xt_st, 1)

            def modulation(out, w_hi, w_lo, q):
                for k in range(2):
                    pe.matmul(out, cond4[:, 2 * q + k, :], w_hi[:, k, :], start=q == 0 and k == 0, stop=False)
                    mm = pe.matmul(out, cond4[:, 2 * q + k, :], w_lo[:, k, :], start=False, stop=q == 3 and k == 1)
                return mm

            for f in range(NK + ADA_LAG):
                if f < NK:
                    if f == 1:
                        pe.wait_ge(cvec_done, 1)
                    if f >= 2:
                        pe.wait_ge(xt_cp, f - 1)
                    for t in range(NT):
                        tr = pe.transpose(PA[:, (f % 2) * 1024 + t * P:(f % 2) * 1024 + (t + 1) * P],
                                          x_rows[:, t, f * P:(f + 1) * P], ident[:, :])
                    tr.then_inc(xt_ps, 1)
                if 1 <= f <= NK:
                    x_stats(f - 1)
                if f >= ADA_LAG:
                    if f == ADA_LAG:
                        pe.wait_ge(cond_done, 3)
                    for a in (2 * (f - ADA_LAG), 2 * (f - ADA_LAG) + 1):
                        pe.wait_ge(ada_lod, a + 1)
                        if a % 4 == 0 and a >= 8:
                            pe.wait_ge(rows_set, a // 4 - 1)
                        bank_ = (2 + a // 4 % 2) * BANK
                        modulation(PJ[0:4, bank_:bank_ + BANK], ada_hi[:, a % ADA_HI], ada_lo[:, a % ADA_SLOTS], a % 4)\
                            .then_inc(ada_used, 1)
            pe.wait_ge(vec_in, 16 * 12)
            pe.wait_ge(xt_cp, NK)
            for s, n in ((0, ROWS_0), (2, ROWS_2)):
                pe.transpose(PA[:, 1024 + s * P:1024 + s * P + n], vec_rows[0:n, s, :], ident[0:n, 0:n]).then_inc(vec_ps, 1)
            pe.wait_ge(rows_set, ADA_FIRST // 4)
            for a in range(ADA_FIRST):
                mm = pe.matmul(PA[:, 1536 + 2 * a:1536 + 2 * a + 2], mod_rows[0:4, a // 4, a % 4 * P:(a % 4 + 1) * P], pick[0:4, :],
                               start=True, stop=True)
            mm.then_inc(mod_ps, 1)
            pe.wait_ge(past_in, 64)
            for j in range(4):
                for b in range(2):
                    tr = pe.transpose(PA[:, j * PAST + b * P:j * PAST + (b + 1) * P], kc_tok[:, b, j * P:(j + 1) * P], ident[:, :])
            tr.then_inc(kct_ps, 1)

            for k in range(NK):
                pe.wait_ge(hlo_set, k + 1)
                project(0, 1 if k == 0 else None, hh, hl, PJ, 0, k0=k, k1=k + 1, start=k == 0, stop=k == NK - 1,
                        done=tile_ready if k == NK - 1 else None)
            pe.wait_ge(tile_freed, 1)
            pe.wait_ge(kct_cp, 1)
            pe.wait_ge(vec_done, 1)
            for m in range(4):
                if m >= 2:
                    pe.wait_ge(la_abs, m - 1)
                    pe.wait_ge(la_min, m - 1)
                for b in range(2):
                    mm = pe.matmul(PA[:, (m % 2) * 1024 + b * BANK:(m % 2) * 1024 + b * BANK + HALF],
                                   w_alpha[0:32, m * P:(m + 1) * P], z[0:32, b * HALF:(b + 1) * HALF], start=True, stop=True)
                mm.then_inc(la_ps, 1)
            pe.wait_ge(mod_set, 1)
            with pe.Fori(0, 6) as i:
                for b in range(2):
                    pe.wait_ge(tile_freed, i * 2 + b)
                    project((b + 1) % 2, i * 2 + (C_GLA + b + 1), hh, hl, PJ, (b + 1) % 2, done=tile_ready)
            bank_seq = [0]

            def next_bank():
                n = bank_seq[0]
                bank_seq[0] += 1
                if n >= 4:
                    pe.wait_ge(lv_cp, n - 3)
                return (n % 4) * BANK

            def v_rows():
                pe.wait_ge(tile_freed, 9)
                pe.wait_ge(la_abs, 4)
                pe.wait_ge(la_min, 4)
                for t in range(NT):
                    at_ = next_bank()
                    for f in range(4):
                        tr = pe.transpose(PA[:, at_ + f * P:at_ + (f + 1) * P], U[:, 4 + f, t * P:(t + 1) * P], ident[:, :])
                    tr.then_inc(vt_ps, 1)

            def level(n):
                w = n % 2
                pe.wait_ge(lv_set, n + 1)
                for r in range(2):
                    for t0 in (0, 2, 4):
                        at_ = next_bank()
                        for t in range(t0, min(t0 + 2, NT)):
                            for dt in range(2):
                                o = at_ + ((t - t0) * 2 + dt) * P
                                mm = pe.matmul(PA[:, o:o + P], lvl[64 * r:64 * r + 64, w, 2 + dt, t * P:(t + 1) * P],
                                               lvl[64 * r:64 * r + 64, w, dt, t * P:(t + 1) * P], start=True, stop=True)
                        mm.then_inc(lv_ps, 1)

            def key_rows():
                for d in range(2):
                    pe.wait_ge(lv_set, N_LEVEL + d + 1)
                    for t0 in (0, 2, 4):
                        at_ = next_bank()
                        for t in range(t0, min(t0 + 2, NT)):
                            for dt in range(2):
                                o = at_ + ((t - t0) * 2 + dt) * P
                                tr = pe.transpose(PA[:, o:o + P], lvl[:, d, 2 + dt, t * P:(t + 1) * P], ident[:, :])
                        tr.then_inc(kt_ps, 1)

            for a in range(12):
                n = C_NA + a
                pe.wait_ge(tile_freed, n - 1)
                project(n % 2, n + 1, hh, hl, PJ, n % 2, done=tile_ready)
                if a == 0:
                    v_rows()
                elif a <= N_LEVEL:
                    level(a - 1)
                elif a == 10:
                    key_rows()
            base_cp = bank_seq[0]
            pe.wait_ge(lv_cp, base_cp)
            for s in range(4):
                for d in range(2):
                    t = NT - 1 if s == 3 else (s if d == 0 else 3 - s)
                    for hd in range(GH):
                        dt, r = hd // 2, hd % 2
                        o = s * BANK + d * 256 + dt * P
                        mm = pe.matmul(PA[64 * r:64 * r + 64, o:o + P],
                                       kt[:, d, t, dt * P + 64 * r:dt * P + 64 * r + 64],
                                       v_tok[:, t, hd * DV:(hd + 1) * DV], start=True, stop=True)
                mm.then_inc(kv_ps, 1)
            pe.wait_ge(tile_freed, C_NA + 12)
            pe.wait_ge(s_set, 12)
            pe.wait_ge(s_copied, 1)
            for t in range(NT):
                if t == 4:
                    pe.wait_ge(nvt_cp, 1)
                for f in range(4):
                    tr = pe.transpose(PA[:, (t % 4) * BANK + f * P:(t % 4) * BANK + (f + 1) * P],
                                      nvraw[:, f, t * P:(t + 1) * P], ident[:, :])
                tr.then_inc(nvt_ps, 1)
            pe.wait_ge(nvt_cp, NT)
            g = 0
            for r in range(2):
                for t0 in (0, 2, 4):
                    if g >= 4:
                        pe.wait_ge(o_cp, g - 3)
                    for t in range(t0, min(t0 + 2, NT)):
                        for dt in range(2):
                            hd = 2 * dt + r
                            o = (g % 4) * BANK + ((t - t0) * 2 + dt) * P
                            mm = pe.matmul(PA[:, o:o + P], v_tok[:, t, hd * DV:(hd + 1) * DV], A[:, r, t, dt, :],
                                           start=True, stop=t == NT - 1)
                            if t < NT - 1:
                                for d in range(2):
                                    mm = pe.matmul(PA[:, o:o + P], S[64 * r:64 * r + 64, d, t, dt, :],
                                                   lvl[64 * r:64 * r + 64, d, dt, t * P:(t + 1) * P],
                                                   start=False, stop=d == 1)
                    mm.then_inc(o_ps, 1)
                    g += 1
            pe.wait_ge(o_cp, 6)
            for hd in range(GH):
                pe.wait_ge(og_sqd, hd + 1)
                if hd >= 2:
                    pe.wait_ge(og_ln, hd - 1)
                for b in range(2):
                    mm = pe.matmul(PA[:, (hd % 2) * 1024 + b * BANK:(hd % 2) * 1024 + b * BANK + HALF], ones[:, :],
                                   og_sq[:, hd % 2, b * HALF:(b + 1) * HALF], start=True, stop=True)
                mm.then_inc(og_st, 1)
            pe.wait_ge(og_ln, 4)

            with pe.Fori(0, 4) as j:
                pe.wait_ge(sq_set, j * 2 + 2)
                pe.wait_ge(pv_cp, j * 10)
                for x in range(2):
                    for b in range(2):
                        mm = pe.matmul(PA[:, (2 * x + b) * BANK:(2 * x + b) * BANK + HALF], blk64[:, :],
                                       qk_rs[:, x, b * HALF:(b + 1) * HALF], start=True, stop=True)
                mm.then_inc(sq_ps, 1)
                pe.wait_ge(qk_set, j * 2 + 2)
                pe.transpose(PA[:, 1024:1024 + P], qk_n[:, 1, SAMPLE:TOK], ident[:, :]).then_inc(ko_ps, 1)
                pe.wait_ge(kcp_set, j + 1)
                for m in range(11):
                    if m < 10:
                        r, i = m // 5, m % 5
                        hs = slice(64 * r, 64 * r + 64)
                        pe.wait_ge(sc_cp, j * 10 + m)
                        if m >= 3:
                            pe.wait_ge(pv_cp, j * 10 + (m - 2))
                        q = qk_n[hs, 0, i * P:(i + 1) * P]
                        if i < 4:
                            t0, nt, _ = KEYS[i]
                            pe.matmul(PA[:, 0:nt * P], q, qk_n[hs, 1, t0 * P:(t0 + nt) * P], start=True, stop=True)
                            pe.matmul(PA[:, BANK:BANK + PAST], q, kc_pair[hs, :], start=True, stop=True).then_inc(sc_ps, 1)
                        else:
                            pe.matmul(PA[:, 0:P], q, qk_n[hs, 1, SAMPLE:TOK], start=True, stop=True).then_inc(sc_ps, 1)
                    if m >= 1:
                        i = (m - 1) % 5
                        nb = KEYS[i][1] + 2 if i < 4 else 1
                        pe.wait_ge(sc_exp, j * 10 + m)
                        if m >= 2:
                            pe.wait_ge(pt_cp, j * 10 + (m - 1))
                        else:
                            pe.wait_ge(ko_cp, j + 1)
                        for b in range(nb):
                            tr = pe.transpose(PA[:, 1024 + b * P:1024 + (b + 1) * P],
                                              sc[:, (m - 1) % 2, b * P:(b + 1) * P], ident[:, :])
                        tr.then_inc(pt_ps, 1)
                    if m < 8:
                        b = m // 4
                        k = 2 * (m % 4)
                        if k == 0:
                            pe.wait_ge(gate_cp, j * 2)
                        project((b + 1) % 2, j * 2 + (C_MG + b + 1) if k == 0 else None, hh, hl, PJ, (b + 1) % 2,
                                k0=k, k1=k + 2, start=k == 0, stop=k == 6, done=tile_ready if k == 6 else None)
                    if m >= 1:
                        r, i = (m - 1) // 5, (m - 1) % 5
                        pe.wait_ge(pt_cp, j * 10 + m)
                        if m >= 2:
                            pe.wait_ge(pv_cp, j * 10 + (m - 1))
                        else:
                            pe.wait_ge(sc_cp, j * 10 + (m + 1))
                        o = BANK + 256 + 64 * ((m - 1) % 2)
                        col = j * 128 + r * 64
                        if i < 4:
                            t0, nt, _ = KEYS[i]
                            vs = [nv_tok[:, t0 + b, bass.ds(col, HD)] for b in range(nt)] + \
                                 [vc[:, b, bass.ds(col, HD)] for b in range(2)]
                        else:
                            vs = [nv_tok[:, 4, bass.ds(col, HD)]]
                        for b, v in enumerate(vs):
                            mm = pe.matmul(PA[:, o:o + HD], pT[:, (m - 1) % 2, b * P:(b + 1) * P], v,
                                           start=b == 0, stop=b == len(vs) - 1)
                        mm.then_inc(pv_ps, 1)
            pe.wait_ge(pv_cp, 40)
            for f in range(4):
                if f >= 2:
                    pe.wait_ge(on_lo, f - 1)
                for t in range(NT):
                    tr = pe.transpose(PA[:, (f % 2) * 1024 + t * P:(f % 2) * 1024 + (t + 1) * P],
                                      o_tok[:, t, f * P:(f + 1) * P], ident[:, :])
                tr.then_inc(on_ps, 1)
            pe.wait_ge(on_lo, 4)
            pe.wait_ge(og_lod, 4)
            pe.wait_ge(gate_cp, NK)
            def rest(j, pieces_):
                for a in pieces_:
                    pe.wait_ge(ada2_lod, j * 4 + (a + 1))
                    modulation(PA[0:4, 1024:1536], ada_rest_hi[:, a % 2], ada_rest_lo[:, a], a).then_inc(ada2_used, 1)

            with pe.Fori(0, NK) as j:
                pe.wait_ge(sn_set, j)
                project(1, j * 2 + C_POST + 1, hh, hl, PJ, 0, done=mna_ps)
                rest(j, (0, 1))
                pe.wait_ge(t1_set, j)
                project(0, j * 2 + C_POST + 2, lambda k: og_hi[:, k, :], lambda k: og_lo[:, k, :], PJ, 1, k1=4, done=bg_ps)
                rest(j, (2, 3))
                pe.wait_ge(t2_set, j)
                project(0, None, lambda k: ona_hi[:, k, :], lambda k: ona_lo[:, k, :], PA, 0, k1=4, w0=4, done=bn_ps)
                pe.wait_ge(ada2_rows, j + 1)
                pe.wait_ge(ada2_cp, j)
                for a in range(4):
                    mm = pe.matmul(PA[:, 1536 + 2 * a:1536 + 2 * a + 2], rest_rows[0:4, a * P:(a + 1) * P], pick[0:4, :],
                                   start=True, stop=True)
                mm.then_inc(ada2_ps, 1)
            pe.wait_ge(mixlo_set, NK)
            pe.wait_ge(ada2_cp, NK)
            pe.wait_ge(zero_set, 2)
            for b in range(2):
                pe.matmul(PA[:, (2 + b) * BANK:(2 + b) * BANK + HALF], ones[:, :], zeros[:, :], start=True, stop=False)

            def x2_stats(slot, stop):
                for b in range(2):
                    mm = pe.matmul(PA[:, (2 + b) * BANK:(2 + b) * BANK + HALF], ones[:, :],
                                   x2_sq[:, slot, b * HALF:(b + 1) * HALF], start=False, stop=stop)
                mm.then_inc(x2_st, 1)

            mh = lambda k: mix_hi[:, k, :]
            ml = lambda k: mix_lo[:, k, :]
            with pe.Fori(0, 4) as i:
                for b in range(2):
                    if b == 0:
                        pe.wait_ge(x2_set, i * 2)
                    project((b + 1) % 2, i * 2 + (C_OUT + b + 1), mh, ml, PJ, b, done=out_ps)
                    pe.wait_ge(xc_in[b], i * 32 + 32)
                    pe.wait_ge(xc_cp, i * 2 + b)
                    for t in range(NT):
                        tr = pe.transpose(PA[:, t * P:(t + 1) * P], x_cols[:, b, t, :], ident[:, :])
                    tr.then_inc(xc_ps, 1)
                    pe.wait_ge(x2_sqd, i * 2 + b)
                    x2_stats((b + 1) % 2, False)
            pe.wait_ge(x2_sqd, NK)
            x2_stats(1, True)

            pe.wait_ge(h2lo_set, NK)
            with pe.Fori(0, NF) as j:
                pe.wait_ge(ua_set, j)
                project(1, j * 2 + (C_UP + 1), hh, hl, PJ, 0, done=up_ps)
                pe.wait_ge(ug_set, j)
                project(0, j * 2 + (C_UP + 2), hh, hl, PJ, 1, done=up_ps)
            pe.wait_ge(actlo_set, NF)
            with pe.Fori(0, 4) as i:
                for b in range(2):
                    pe.wait_ge(y_set, i * 2)
                    k0 = 0
                    for q in range(3):
                        n = 3 * b + q
                        project((n + 1) % 2, i * 6 + (C_DOWN + n + 1), lambda k, k0=k0: act_hi[:, k0 + k, :],
                                lambda k, k0=k0: act_lo[:, k0 + k, :], PJ, b, k1=DOWN_K[q],
                                start=q == 0, stop=q == 2, done=dn_ps)
                        k0 += DOWN_K[q]
                        if n == 3:
                            pe.wait_ge(y_set, i * 2 + 1)
                            pe.wait_ge(y_cp, i * 2)
                            for t in range(NT):
                                tr = pe.transpose(PA[:, t * P:(t + 1) * P], yT[:, 0, t * P:(t + 1) * P], ident[:, :])
                            tr.then_inc(yt_ps, 1)
                pe.wait_ge(y_set, i * 2 + 2)
                for t in range(NT):
                    tr = pe.transpose(PA[:, 1024 + t * P:1024 + (t + 1) * P], yT[:, 1, t * P:(t + 1) * P], ident[:, :])
                tr.then_inc(yt_ps, 1)

        def level_view(x, w):
            return lvl[:, x[0], 2 * x[1]:2 * x[1] + 2, :].rearrange("p d (t a b c) -> p (d t a) b c", t=NT, b=2, c=w)

        def y_view(d):
            return Y[:, 2 * d:2 * d + 2, :, :].rearrange("p d t n -> p (d t) n")

        @block.scalar
        def _(act):
            def on_constant():
                act.wait_ge(const_set, 4)

            def hi(slot, loaded):
                act.wait_ge(raw_in[slot], loaded * 32)
                act.activation(whi[:, slot, :, :], wraw[:, slot, :, :], ACT.Copy).then_inc(hi_done, 1)

            conv = w_conv[0].rearrange("t (r n) -> t r n", n=P)
            act.dma_start(vec_rows[V_C:V_C + 8, 1, :], c[0].rearrange("(r n) -> r n", n=P)).then_inc(cvec_in, 16)
            act.dma_start(vec_rows[V_CCTX:V_CCTX + 8, 1, :], c_ctx.rearrange("(r n) -> r n", n=P)).then_inc(cvec_in, 16)
            act.dma_start(pick[0:4, :], tables[0:4, 1280:1282]).then_inc(tab_in, 16)
            act.dma_start(vec_rows[0:88, 1, :], conv[1:3].rearrange("t r n -> (t r) n")).then_inc(cvec_in, 16)
            for v, at_, n in ((w_conv[0, 0], V_W0, 44), (b_ada[0], V_BADA, 48), (g_mix[0], V_GMIX, 8), (g_ffn[0], V_GFFN, 8),
                              (b_af[0], V_BAF, 2), (b_ab[0], V_BAB, 2), (g_gla[0], V_GGLA, 1)):
                act.dma_start(vec_rows[at_:at_ + n, 0, :], v.rearrange("(r n) -> r n", n=P)).then_inc(vec_in, 16)
            act.dma_start(vec_rows[0:44, 2, :], b_conv[0].rearrange("(r n) -> r n", n=P)).then_inc(vec_in, 16)
            for v, at_, o in ((g_q[0], V_GQ, 0), (g_k[0], V_GK, 0), (g_q[0], V_GQ, 64), (g_k[0], V_GK, 64)):
                act.dma_start(vec_rows[at_:at_ + 1, 0, o:o + HD], v.rearrange("(r n) -> r n", n=HD)).then_inc(vec_in, 16)
            act.wait_ge(cvec_done, 1)
            act.activation(cond_sig[:, :], vec[:, 1, V_C:V_C + 16], ACT.Sigmoid).then_inc(cond_sg, 1)
            act.wait_ge(const_set, 4)
            for f in range(NK + ADA_LAG):
                if f < NK:
                    act.wait_ge(xt_cp, f + 1)
                    if f >= 2:
                        act.wait_ge(xt_st, f - 1)
                    act.activation(x_sq[:, f % 2, :], xT[:, f, :], ACT.Square).then_inc(xt_sq, 1)
                if f >= ADA_LAG:
                    for a in (2 * (f - ADA_LAG), 2 * (f - ADA_LAG) + 1):
                        act.wait_ge(ada_in[a % ADA_SLOTS], 16 * (a // ADA_SLOTS + 1))
                        if a >= ADA_HI:
                            act.wait_ge(ada_used, a - ADA_HI + 1)
                        act.activation(ada_hi[:, a % ADA_HI], ada_first[:, a % ADA_SLOTS], ACT.Copy).then_inc(ada_hid, 1)
            act.wait_ge(xt_st, NK)
            act.activation(by_half(rstd[:, :]), halves(PJ, 0), ACT.Ln, bias=eps[:, :], scale=1.0 / D).then_inc(rs_ln, 1)
            act.wait_ge(rs_ln, 1)
            act.activation(rstd[:, :], rstd[:, :], ACT.Exp, scale=-0.5).then_inc(rs_done, 1)
            act.wait_ge(kct_ps, 1)
            act.activation(kcT[:, :, :].rearrange("p a b -> p (a b)"), PA[:, 0:1024], ACT.Copy).then_inc(kct_cp, 1)
            act.wait_ge(rpb_moved, 16 * GC)
            act.dma_start(window[:, :], tables[:, 384:384 + 896]).then_inc(mask_in, 16)
            act.dma_start(level_mask[:, :, :].bitcast(I32), level_masks).then_inc(mask_in, 16)
            hi(0, 1)
            for k in range(NK):
                act.wait_ge(hf_set, k + 1)
                act.activation(h_hi[:, k, :], h_f[:, k % 2, :], ACT.Copy).then_inc(hhi_set, 1)
            hi(1, 1)
            act.wait_ge(bias8_set, 1)
            act.wait_ge(tile_ready, 1)
            hi(0, 2)
            act.activation(by_half(z[0:32, :]), halves(PJ, 0)[0:32], ACT.Copy).then_inc(tile_freed, 1)
            for m in range(4):
                act.wait_ge(la_ps, m + 1)
                act.activation(by_half(la_e[:, m, :]), halves(PA, m % 2), ACT.Abs,
                               bias=vec[:, 0, V_BAF + m:V_BAF + m + 1]).then_inc(la_abs, 1)
                act.wait_ge(la_abs, m + 1)
                act.activation(la_e[:, m, :], la_e[:, m, :], ACT.Exp, scale=-1.0).then_inc(la_exp, 1)
                act.wait_ge(la_exp, m + 1)
                act.activation(la_e[:, m, :], la_e[:, m, :], ACT.Ln, bias=one[:, :]).then_inc(la_ln, 1)
            with act.Fori(0, 6) as i:
                for b in range(2):
                    act.wait_ge(tile_ready, i * 2 + (b + 2))
                    hi((b + 1) % 2, i + (2 + b))
                    act.activation(by_half(U[:, bass.ds(i * 2 + b, 1), :].rearrange("p a n -> p (a n)")),
                                   halves(PJ, (b + 1) % 2), ACT.Copy).then_inc(tile_freed, 1)
            act.wait_ge(tile_freed, 13)
            act.activation(U[:, 8:12, :], U[:, 8:12, :], ACT.Silu).then_inc(gr_silu, 1)
            for a in range(12):
                n = C_NA + a
                act.wait_ge(tile_ready, n + 1)
                hi(n % 2, (n + 2) // 2 + 1)
                dst = nqk[:, a, :] if a < 8 else nvraw[:, a - 8, :]
                grouped = dst[:, 0:SAMPLE].rearrange("p (g r c) -> p r g c", g=4, c=GC)
                ps = halves(PJ, n % 2)
                act.activation(grouped[:, 0:5], ps[:, 0, :].rearrange("p (r g c) -> p r g c", g=4, c=GC), ACT.Copy)
                act.activation(grouped[:, 5:8], ps[:, 1, 0:192].rearrange("p (r g c) -> p r g c", g=4, c=GC), ACT.Copy)
                act.activation(dst[:, SAMPLE:TOK], ps[:, 1, 192:HALF], ACT.Copy).then_inc(tile_freed, 1)
                if a < 9:
                    lv = a + 1
                    act.wait_ge(lv_arg, lv)
                    act.activation(lvl[:, lv % 2, :, :], lvl[:, lv % 2, :, :], ACT.Exp, scale=1.0 / 16).then_inc(lv_exp, 1)
                if a == 9:
                    act.activation(decay[:, :, :], Y[:, :, :, P:P + 1].rearrange("p m t o -> p m (t o)"), ACT.Exp,
                                   scale=1.0 / 16).then_inc(decay_set, 1)
            act.wait_ge(decay_set, 1)
            for d, st in enumerate((state_f, state_b)):
                act.dma_start(S[:, d, 3 * d, :, :], st[0, 0].rearrange("(t r) d v -> (r d) t v", r=2)).then_inc(s0_in, 16)
            act.wait_ge(s_copied, 1)
            for d, st in enumerate((new_sf, new_sb)):
                act.dma_start(st[0, 0].rearrange("(t r) d v -> (r d) t v", r=2), s_out[:, d, :, :]).then_inc(s_stored, 16)
            act.wait_ge(nvt_cp, NT)
            act.dma_start(new_v[0, 0].rearrange("s h d -> s (h d)"), nv_tok[:, NT - 1, :]).then_inc(nv_stored, 16)
            g = 0
            o_v = oT[:, :, :].rearrange("p (dt r) (t n) -> p r t dt n", r=2, n=P)
            for r in range(2):
                for t0 in (0, 2, 4):
                    nt = min(2, NT - t0)
                    act.wait_ge(o_ps, g + 1)
                    act.activation(o_v[:, r, t0:t0 + nt], PA[:, (g % 4) * BANK:(g % 4) * BANK + nt * 256]
                                   .rearrange("p (t dt n) -> p t dt n", dt=2, n=P), ACT.Copy).then_inc(o_cp, 1)
                    g += 1
            act.wait_ge(o_cp, 6)

            def gla_square(hd):
                act.activation(og_sq[:, hd % 2, :], oT[:, hd, :], ACT.Square).then_inc(og_sqd, 1)

            gla_square(0)
            gla_square(1)
            for hd in range(GH):
                act.wait_ge(og_st, hd + 1)
                if hd >= 2:
                    act.wait_ge(og_n, hd - 1)
                act.activation(by_half(og_rs[:, hd % 2, :]), halves(PA, hd % 2), ACT.Ln, bias=eps[:, :],
                               scale=1.0 / DV).then_inc(og_ln, 1)
                act.wait_ge(og_ln, hd + 1)
                act.activation(og_rs[:, hd % 2, :], og_rs[:, hd % 2, :], ACT.Exp, scale=-0.5).then_inc(og_rsd, 1)
                if hd + 2 < GH:
                    gla_square(hd + 2)
            for hd in range(GH):
                act.wait_ge(og_g, hd + 1)
                act.activation(og_hi[:, hd, :], oT[:, hd, :], ACT.Copy).then_inc(og_hid, 1)
            act.wait_ge(og_lod, GH)

            with act.Fori(0, 4) as j:
                on_constant()
                act.wait_ge(qk_set, j * 2)
                for x in range(2):
                    act.activation(qk_rs[:, x:x + 1, :], nqk[:, bass.ds(j + 4 * x, 1), :], ACT.Square).then_inc(sq_set, 1)
                act.wait_ge(sq_ps, j + 1)
                act.activation(qk_rs[:, :, :].rearrange("p x (b n) -> p (x b) n", b=2),
                               PA[:, :].rearrange("p (b n) -> p b n", b=4)[:, :, 0:HALF], ACT.Ln,
                               bias=eps[:, :], scale=1.0 / HD).then_inc(sq_ln, 1)
                act.wait_ge(sq_ln, j + 1)
                act.activation(qk_rs[:, :, :], qk_rs[:, :, :], ACT.Exp, scale=-0.5).then_inc(sq_rs, 1)
                on_constant()
                act.wait_ge(sc_ps, j * 10)
                act.activation(kc_pair[:, :].unsqueeze(1), kcT[:, bass.ds(j, 1), :], ACT.Copy).then_inc(kcp_set, 1)
                act.wait_ge(ko_ps, j + 1)
                act.wait_ge(ko_stored, j * 16)
                act.activation(k_out[:, :], PA[:, 1024:1024 + P], ACT.Copy).then_inc(ko_cp, 1)
                act.wait_ge(ko_cp, j + 1)
                act.dma_start(new_k[0, 0].rearrange("s h d -> s (h d)")[:, bass.ds(j * P, P)], k_out[:, :])\
                   .then_inc(ko_stored, 16)
                for m in range(11):
                    if m >= 1:
                        i = (m - 1) % 5
                        n = (KEYS[i][1] + 2) * P if i < 4 else P
                        act.wait_ge(pt_ps, j * 10 + m)
                        if m >= 3:
                            act.wait_ge(pv_ps, j * 10 + (m - 2))
                        act.activation(pT[:, (m - 1) % 2, 0:n], PA[:, 1024:1024 + n], ACT.Copy).then_inc(pt_cp, 1)
                    if m < 10:
                        i = m % 5
                        n = (KEYS[i][1] + 2) * P if i < 4 else P
                        act.wait_ge(sc_cp, j * 10 + (m + 1))
                        act.activation(sc[:, m % 2, 0:n], sc[:, m % 2, 0:n], ACT.Exp, bias=nmx[:, m:m + 1],
                                       accum_out=psm[:, m:m + 1]).then_inc(sc_exp, 1)
                    if m in (4, 8):
                        b = m // 4 - 1
                        act.wait_ge(tile_ready, j * 2 + (C_MG + b + 1))
                        hi((b + 1) % 2, j + (14 + b))
                        act.activation(by_half(sg[:, bass.ds(j * 2 + b, 1), :].rearrange("p a n -> p (a n)")),
                                       halves(PJ, (b + 1) % 2), ACT.Sigmoid).then_inc(gate_cp, 1)
            for f in range(4):
                act.wait_ge(on_ps, f + 1)
                ps = PA[:, (f % 2) * 1024:(f % 2) * 1024 + TOK]
                act.activation(ona_hi[:, f, 0:SAMPLE].rearrange("p (r g c) -> p r g c", g=4, c=GC),
                               ps[:, 0:SAMPLE].rearrange("p (g r c) -> p r g c", g=4, c=GC), ACT.Copy)
                act.activation(ona_hi[:, f, SAMPLE:TOK], ps[:, SAMPLE:TOK], ACT.Copy).then_inc(on_hi, 1)
            def rest_hi(j, a):
                act.wait_ge(ada2_in[a], j * 16 + 16)
                act.wait_ge(ada2_used, j * 4 + max(a - 1, 0))
                act.activation(ada_rest_hi[:, a % 2], ada_rest[:, a], ACT.Copy).then_inc(ada2_hid, 1)

            with act.Fori(0, NK) as j:
                rest_hi(j, 0)
                rest_hi(j, 1)
                act.wait_ge(mna_ps, j + 1)
                hi(1, j + 18)
                act.wait_ge(t2_set, j)
                act.activation(by_half(sn[:, :]), halves(PJ, 0), ACT.Sigmoid).then_inc(sn_set, 1)
                rest_hi(j, 2)
                rest_hi(j, 3)
                act.wait_ge(bn_ps, j + 1)
                hi(0, j + 19)
                on_constant()
                act.wait_ge(mixf_set, j + 1)
                act.activation(mix_hi[:, bass.ds(j, 1), :], t1[:, :].unsqueeze(1), ACT.Copy).then_inc(mixhi_set, 1)
            with act.Fori(0, 4) as i:
                for b in range(2):
                    act.wait_ge(out_ps, i * 2 + (b + 1))
                    hi((b + 1) % 2, i + (26 + b))
                    on_constant()
                    act.wait_ge(xc_ps, i * 2 + (b + 1))
                    act.activation(x2[:, bass.ds(i * 2 + b, 1), :], PA[:, 0:TOK].unsqueeze(1), ACT.Copy).then_inc(xc_cp, 1)
                    on_constant()
                    act.wait_ge(x2_set, i * 2 + (b + 1))
                    act.wait_ge(x2_st, i * 2 + b)
                    act.activation(x2_sq[:, b:b + 1, :], x2[:, bass.ds(i * 2 + b, 1), :], ACT.Square).then_inc(x2_sqd, 1)
            act.wait_ge(x2_st, NK + 1)
            act.activation(by_half(rstd2[:, :]), halves(PA, 1), ACT.Ln, bias=eps[:, :], scale=1.0 / D).then_inc(rs2_ln, 1)
            act.wait_ge(rs2_ln, 1)
            act.activation(rstd2[:, :], rstd2[:, :], ACT.Exp, scale=-0.5).then_inc(rs2_done, 1)
            for k in range(NK):
                act.wait_ge(h2f_set, k + 1)
                act.activation(h_hi[:, k, :], h2_f[:, k % 2, :], ACT.Copy).then_inc(h2hi_set, 1)
            act.wait_ge(pad_set, 2)
            with act.Fori(0, NF) as j:
                for b, (u, step, done) in enumerate(((ua, ca_step, ua_set), (ug, cg_step, ug_set))):
                    act.wait_ge(up_ps, j * 2 + (b + 1))
                    hi((b + 1) % 2, j + (30 + b))
                    act.wait_ge(step, j * 3)
                    ps = halves(PJ, b)
                    act.activation(u[:, 1:1 + HALF], ps[:, 0, :], ACT.Copy)
                    act.activation(u[:, 1 + HALF:1 + SAMPLE], ps[:, 1, 0:SAMPLE - HALF], ACT.Copy)
                    act.activation(u[:, 2 + SAMPLE:2 + TOK], ps[:, 1, SAMPLE - HALF:HALF], ACT.Copy).then_inc(done, 1)
                act.wait_ge(cg_step, j * 3 + 3)
                act.activation(cg[:, :], cg[:, :], ACT.Silu).then_inc(silu_set, 1)
                on_constant()
                act.wait_ge(prod_set, j + 1)
                act.activation(act_hi[:, bass.ds(j, 1), 0:SAMPLE], ca[:, 0:SAMPLE].unsqueeze(1), ACT.Copy)
                act.activation(act_hi[:, bass.ds(j, 1), SAMPLE:TOK], ca[:, SAMPLE + 1:TOK + 1].unsqueeze(1), ACT.Copy)\
                   .then_inc(acthi_set, 1)

            def down(i, last):
                for n in range(6):
                    act.wait_ge(dn_ps, i * 6 + (n + 1))
                    if not (last and n >= 4):
                        hi((n + 1) % 2, i * 3 + ((C_DOWN + 2 + n) // 2 + 1))
                    if n in (3, 5):
                        b = 0 if n == 3 else 1
                        act.wait_ge(yt_ps, i * 2 + (b + 1))
                        act.wait_ge(y_stored, i * 64)
                        act.activation(y_tok[:, b, :, :].rearrange("p t n -> p (t n)"), PA[:, b * 1024:b * 1024 + TOK],
                                       ACT.Copy).then_inc(y_cp, 1)
                        act.wait_ge(y_cp, i * 2 + (b + 1))
                        act.dma_start(ys_v[:, :, bass.ds(i * 256 + b * P, P)], y_tok[:, b, 0:4, :]).then_inc(y_stored, 16)
                        act.dma_start(y_prompt[0][:, bass.ds(i * 256 + b * P, P)], y_tok[:, b, 4, :]).then_inc(y_stored, 16)

            with act.Fori(0, 3) as i:
                down(i, False)
            down(3, True)
            act.wait_ge(y_stored, 16 * 16)
            act.wait_ge(ko_stored, 4 * 16)
            act.wait_ge(s_stored, 2 * 16)
            act.wait_ge(nv_stored, 16)

        @block.vector
        def _(dve):
            def bc(ap, shape):
                return ap.to_broadcast(shape)

            def on_constant():
                dve.wait_ge(const_set, 4)

            dve.memset(eps[:, :], EPS).then_inc(const_set, 1)
            dve.memset(one[:, :], 1.0).then_inc(const_set, 1)
            dve.memset(w_alpha[:, :], 0.0).then_inc(const_set, 1)
            dve.memset(rpb_wide[:, :, :, :], 0.0).then_inc(const_set, 1)
            dve.wait_ge(vec_ps, 1)
            dve.tensor_copy(vec[:, 1, 0:ROWS_1], PA[:, 1024:1024 + ROWS_1]).then_inc(cvec_done, 1)
            dve.wait_ge(cvec_done, 1)
            dve.wait_ge(cond_sg, 1)
            dve.tensor_tensor(cond[:, :, :].rearrange("p a b -> p (a b)"), vec[:, 1, V_C:V_C + 16], cond_sig[:, :],
                              ALU.mult).then_inc(cond_done, 1)
            dve.wait_ge(cond_done, 1)
            by_vector = cond[:, :, :].rearrange("p a k -> p k a")
            dve.tensor_copy(cond4[:, :, 0:2], by_vector).then_inc(cond_done, 1)
            dve.wait_ge(cond_done, 2)
            dve.tensor_tensor(cond4[:, :, 2:4], by_vector, cond4[:, :, 0:2].bitcast(F32), ALU.subtract).then_inc(cond_done, 1)

            def rows_out(g):
                dve.wait_ge(ada_used, 4 * g + 4)
                dve.tensor_copy(mod_rows[0:4, g, :], PJ[0:4, (2 + g % 2) * BANK:(3 + g % 2) * BANK]).then_inc(rows_set, 1)

            for f in range(NK + ADA_LAG):
                if f < NK:
                    dve.wait_ge(xt_ps, f + 1)
                    dve.tensor_copy(xT[:, f, :], PA[:, (f % 2) * 1024:(f % 2) * 1024 + TOK]).then_inc(xt_cp, 1)
                if f >= ADA_LAG:
                    for a in (2 * (f - ADA_LAG), 2 * (f - ADA_LAG) + 1):
                        dve.wait_ge(ada_hid, a + 1)
                        dve.tensor_tensor(ada_lo[:, a % ADA_SLOTS], ada_first[:, a % ADA_SLOTS],
                                          ada_hi[:, a % ADA_HI].bitcast(F32), ALU.subtract).then_inc(ada_lod, 1)
                    if f - ADA_LAG >= 2 and (f - ADA_LAG) % 2 == 0:
                        rows_out((f - ADA_LAG) // 2 - 1)
            rows_out(3)
            dve.wait_ge(vec_ps, 3)
            dve.tensor_copy(vec[:, 0, 0:ROWS_0], PA[:, 1024:1024 + ROWS_0])
            dve.tensor_copy(vec[:, 2, 0:ROWS_2], PA[:, 1024 + 2 * P:1024 + 2 * P + ROWS_2]).then_inc(vec_done, 1)
            dve.wait_ge(vec_done, 1)
            dve.wait_ge(mod_ps, 1)
            dve.tensor_tensor(mod[:, 0:ADA_FIRST, :], PA[:, 1536:1536 + 2 * ADA_FIRST].rearrange("p (a c) -> p a c", c=2),
                              bc(vec[:, 0, V_BADA:V_BADA + ADA_FIRST].unsqueeze(2), [P, ADA_FIRST, 2]), ALU.add)\
               .then_inc(mod_set, 1)
            dve.wait_ge(mod_set, 1)
            dve.tensor_scalar(a1[:, :, :], mod[:, NK:2 * NK, :], 1.0, None, ALU.add).then_inc(a1_set, 1)
            dve.wait_ge(a1_set, 1)
            dve.tensor_tensor(a1[:, :, :], a1[:, :, :], bc(vec[:, 0, V_GMIX:V_GMIX + NK].unsqueeze(2), [P, NK, 2]),
                              ALU.mult).then_inc(a1_set, 1)

            def modulated(src, rs, t, f, sc_, sh, t_set, f_set, hi_set, lo_set):
                def low(k):
                    dve.wait_ge(hi_set, k + 1)
                    dve.tensor_tensor(h_lo[:, k, :], f[:, k % 2, :], h_hi[:, k, :].bitcast(F32), ALU.subtract)\
                       .then_inc(lo_set, 1)
                for k in range(NK):
                    if k >= 1:
                        dve.wait_ge(f_set, k)
                    dve.tensor_tensor(t[:, :], src[:, k, :], rs[:, :], ALU.mult).then_inc(t_set, 1)
                    dve.wait_ge(t_set, k + 1)
                    if k >= 2:
                        dve.wait_ge(lo_set, k - 1)
                    dve.tensor_scalar(f[:, k % 2, 0:SAMPLE], t[:, 0:SAMPLE], sc_[:, k, 0:1], sh(k, 0), ALU.mult, ALU.add)
                    dve.tensor_scalar(f[:, k % 2, SAMPLE:TOK], t[:, SAMPLE:TOK], sc_[:, k, 1:2], sh(k, 1), ALU.mult, ALU.add)\
                       .then_inc(f_set, 1)
                    if k >= 1:
                        low(k - 1)
                low(NK - 1)

            dve.wait_ge(a1_set, 2)
            dve.wait_ge(rs_done, 1)
            modulated(xT, rstd, h_t, h_f, a1, lambda k, r: mod[:, k, r:r + 1], ht_set, hf_set, hhi_set, hlo_set)
            dve.memset(Y[:, :, :, 0:1], 0.0).then_inc(const_set, 1)
            for m in range(4):
                dve.wait_ge(la_abs, m + 1)
                dve.tensor_scalar(by_half(la_m[:, m, :]), halves(PA, m % 2), vec[:, 0, V_BAF + m:V_BAF + m + 1], 0.0,
                                  ALU.add, ALU.min).then_inc(la_min, 1)
            for m in range(4):
                dve.wait_ge(la_ln, m + 1)
                dve.wait_ge(la_min, m + 1)
                dve.tensor_tensor(la_m[:, m, :], la_m[:, m, :], la_e[:, m, :], ALU.subtract).then_inc(la_sub, 1)
                dve.wait_ge(la_sub, m + 1)
                for t in range(NT):
                    ins = dve.tensor_tensor_scan(Y[:, m, t, 1:P + 1], ones[:, :], la_m[:, m, t * P:(t + 1) * P], 0.0,
                                                 ALU.mult, ALU.add)
                ins.then_inc(la_sum, 1)
            dve.wait_ge(tile_freed, 3)
            dve.tensor_scalar(U[:, 0:2, :], U[:, 0:2, :], DK ** -0.5, None, ALU.mult).then_inc(q_scaled, 1)
            dve.wait_ge(q_scaled, 1)
            dve.wait_ge(la_sum, 4)
            dve.wait_ge(const_set, 5)
            dve.wait_ge(tile_freed, 5)
            bank_seq = [0]

            def copied(ins):
                ins.then_inc(lv_cp, 1)
                bank_seq[0] += 1

            def bank():
                return (bank_seq[0] % 4) * BANK

            def args(n):
                b = n % 2
                if n >= 2:
                    dve.wait_ge(lv_ps, 6 * min(n - 1, N_LEVEL))
                yf, yb = y_view(0), y_view(1)
                if n < N_LEVEL:
                    w = 64 >> (n - 1)
                    pairs = P // (2 * w)
                    sh = [P, 2 * NT, pairs, w]

                    def tokens(y, first):
                        return y[:, :, first:first + P].rearrange("p m (a b c) -> p m a b c", b=2, c=w)[:, :, :, 0, :]

                    def border(y):
                        v = y[:, :, w:w + P - w + 1:2 * w] if pairs > 1 else y[:, :, w:w + 1]
                        return v.unsqueeze(3).to_broadcast(sh)

                    q = lvl[:, b, 0:2, :].rearrange("p d (t a b c) -> p (d t) a b c", t=NT, b=2, c=w)
                    k = lvl[:, b, 2:4, :].rearrange("p d (t a b c) -> p (d t) a b c", t=NT, b=2, c=w)

                    def later(y, first):
                        if pairs == 1:
                            return y[:, :, first:first + w].unsqueeze(2)
                        return y[:, :, first - w:first - w + P].rearrange("p m (a b c) -> p m a b c", b=2, c=w)[:, :, :, 1, :]

                    dve.tensor_tensor(q[:, :, :, 1, :], later(yf, w + 1), border(yf), ALU.subtract)
                    dve.tensor_tensor(k[:, :, :, 0, :], border(yf), tokens(yf, 1), ALU.subtract)
                    dve.tensor_tensor(q[:, :, :, 0, :], border(yb), tokens(yb, 0), ALU.subtract)
                    dve.tensor_tensor(k[:, :, :, 1, :], later(yb, w), border(yb), ALU.subtract).then_inc(lv_arg, 1)
                else:
                    q = lvl[:, b, 0:2, :].rearrange("p d (t n) -> p (d t) n", n=P)
                    k = lvl[:, b, 2:4, :].rearrange("p d (t n) -> p (d t) n", n=P)
                    if n == N_LEVEL:
                        dve.tensor_copy(q, yf[:, :, 1:P + 1])
                        dve.tensor_tensor(k, bc(yf[:, :, P:P + 1], [P, 2 * NT, P]), yf[:, :, 1:P + 1], ALU.subtract)\
                           .then_inc(lv_arg, 1)
                    else:
                        dve.tensor_tensor(q, bc(yb[:, :, P:P + 1], [P, 2 * NT, P]), yb[:, :, 0:P], ALU.subtract)
                        dve.tensor_copy(k, yb[:, :, 0:P]).then_inc(lv_arg, 1)

            def decayed(n):
                dve.wait_ge(lv_exp, n)
                dve.tensor_tensor(lvl[:, n % 2, :, :], lvl[:, n % 2, :, :], U[:, 0:4, :], ALU.mult).then_inc(lv_set, 1)

            def score_copy(n):
                for r in range(2):
                    for g, t0 in enumerate((0, 2, 4)):
                        nt = min(2, NT - t0)
                        dve.wait_ge(lv_ps, 6 * n + 3 * r + g + 1)
                        copied(dve.copy_predicated(
                            A[:, r, t0:t0 + nt, :, :].rearrange("p t d n -> p (t d) n"),
                            bc(level_mask[:, n, :].unsqueeze(1), [P, 2 * nt, P]),
                            PA[:, bank():bank() + nt * 256].rearrange("p (m n) -> p m n", n=P)))

            dve.tensor_scalar(lvl[:, 0, 0:2, :], U[:, 0:2, :], 2.0, None, ALU.mult)
            dve.tensor_copy(lvl[:, 0, 2:4, :], U[:, 2:4, :]).then_inc(lv_set, 1)
            for t in range(NT):
                dve.wait_ge(vt_ps, t + 1)
                copied(dve.tensor_copy(v_tok[:, t, :], PA[:, bank():bank() + BANK]))
            dve.wait_ge(mask_in, 32)
            for n in range(1, N_LEVEL + 2):
                args(n)
                if n <= N_LEVEL:
                    score_copy(n - 1)
                decayed(n)
            dve.wait_ge(lv_set, N_LEVEL + 2)
            for d in range(2):
                for g, t0 in enumerate((0, 2, 4)):
                    nt = min(2, NT - t0)
                    dve.wait_ge(kt_ps, 3 * d + g + 1)
                    copied(dve.tensor_copy(kt[:, d, t0:t0 + nt, :].rearrange("p t n -> p (t n)"),
                                           PA[:, bank():bank() + nt * 256]))
            dve.wait_ge(s0_in, 32)
            dve.wait_ge(decay_set, 1)
            for s in range(3):
                for d in range(2):
                    dve.wait_ge(kv_ps, s + 1)
                    cur, nxt = (s, s + 1) if d == 0 else (3 - s, 2 - s)
                    if s:
                        dve.wait_ge(s_set, 4 * s)
                    for dt in range(2):
                        o = s * BANK + d * 256 + dt * P
                        dve.scalar_tensor_tensor(out=S[:, d, nxt, dt, :], in0=S[:, d, cur, dt, :],
                                                 scalar=decay[:, 2 * d + dt, cur:cur + 1], in1=PA[:, o:o + P],
                                                 op0=ALU.mult, op1=ALU.add).then_inc(s_set, 1)
            dve.wait_ge(kv_ps, 4)
            dve.tensor_copy(s_out[:, :, :, :].rearrange("p a b n -> p (a b n)"), PA[:, 3 * BANK:4 * BANK]).then_inc(s_copied, 1)
            for t in range(NT):
                dve.wait_ge(nvt_ps, t + 1)
                dve.tensor_copy(nv_tok[:, t, :], PA[:, (t % 4) * BANK:(t % 4 + 1) * BANK]).then_inc(nvt_cp, 1)
            dve.wait_ge(gr_silu, 1)

            def gla_low(hd):
                dve.wait_ge(og_hid, hd + 1)
                dve.tensor_tensor(og_lo[:, hd, :], oT[:, hd, :], og_hi[:, hd, :].bitcast(F32), ALU.subtract)\
                   .then_inc(og_lod, 1)

            for hd in range(GH):
                dve.wait_ge(og_rsd, hd + 1)
                dve.scalar_tensor_tensor(out=oT[:, hd, :], in0=oT[:, hd, :], scalar=vec[:, 0, V_GGLA:V_GGLA + 1],
                                         in1=og_rs[:, hd % 2, :], op0=ALU.mult, op1=ALU.mult).then_inc(og_n, 1)
                dve.wait_ge(og_n, hd + 1)
                dve.tensor_tensor(oT[:, hd, :], oT[:, hd, :], U[:, 8 + hd, :], ALU.mult).then_inc(og_g, 1)
            for hd in range(GH):
                gla_low(hd)

            with dve.Fori(0, 4) as j:
                dve.wait_ge(sq_rs, j + 1)
                dve.wait_ge(sc_ps, j * 10)
                for x, g in ((0, V_GQ), (1, V_GK)):
                    dve.scalar_tensor_tensor(out=qk_n[:, x:x + 1, :], in0=nqk[:, bass.ds(j + 4 * x, 1), :],
                                             scalar=vec[:, 0, g:g + 1], in1=qk_rs[:, x:x + 1, :],
                                             op0=ALU.mult, op1=ALU.mult).then_inc(qk_set, 1)
                dve.wait_ge(bias_set, j * 3 + 3)
                for m in range(12):
                    if m < 10:
                        r, i = m // 5, m % 5
                        dve.wait_ge(sc_ps, j * 10 + (m + 1))
                        if m >= 2:
                            dve.wait_ge(pt_ps, j * 10 + (m - 1))
                        if i < 4:
                            n = KEYS[i][1] * P
                            b0 = KEYS[i][2]
                            dve.tensor_scalar(sc[:, m % 2, n:n + PAST], PA[:, BANK:BANK + PAST], HD ** -0.5, None, ALU.mult,
                                              ALU.max, accum_out=mx[:, 1, m:m + 1])
                            dve.tensor_tensor_reduce(sc[:, m % 2, 0:n], PA[:, 0:n], bias[:, r, b0:b0 + n], HD ** -0.5, -3e38,
                                                     ALU.add, ALU.max, mx[:, 0, m:m + 1]).then_inc(sc_mx, 1)
                            dve.wait_ge(sc_mx, j * 10 + (m + 1))
                            dve.tensor_scalar(nmx[:, m:m + 1], mx[:, 0, m:m + 1], mx[:, 1, m:m + 1], -1.0, ALU.max, ALU.mult)\
                               .then_inc(sc_cp, 1)
                        else:
                            dve.tensor_scalar(sc[:, m % 2, 0:P], PA[:, 0:P], HD ** -0.5, None, ALU.mult,
                                              ALU.max, accum_out=mx[:, 1, m:m + 1]).then_inc(sc_mx, 1)
                            dve.wait_ge(sc_mx, j * 10 + (m + 1))
                            dve.tensor_scalar(nmx[:, m:m + 1], mx[:, 1, m:m + 1], -1.0, None, ALU.mult).then_inc(sc_cp, 1)
                    if m >= 2:
                        q = m - 2
                        r, i = q // 5, q % 5
                        dve.wait_ge(pv_ps, j * 10 + (q + 1))
                        dve.reciprocal(rin[:, q:q + 1], psm[:, q:q + 1]).then_inc(rin_set, 1)
                        dve.wait_ge(rin_set, j * 10 + (q + 1))
                        o = BANK + 256 + 64 * (q % 2)
                        dve.tensor_scalar(o_tok[:, i, bass.ds(j * P + r * HD, HD)], PA[:, o:o + HD], rin[:, q:q + 1], None,
                                          ALU.mult).then_inc(pv_cp, 1)
            dve.wait_ge(ko_stored, 4 * 16)
            for f in range(4):
                dve.wait_ge(on_hi, f + 1)
                ps = PA[:, (f % 2) * 1024:(f % 2) * 1024 + TOK]
                dve.tensor_tensor(ona_lo[:, f, 0:SAMPLE].rearrange("p (r g c) -> p r g c", g=4, c=GC),
                                  ps[:, 0:SAMPLE].rearrange("p (g r c) -> p r g c", g=4, c=GC),
                                  ona_hi[:, f, 0:SAMPLE].bitcast(F32).rearrange("p (r g c) -> p r g c", g=4, c=GC), ALU.subtract)
                dve.tensor_tensor(ona_lo[:, f, SAMPLE:TOK], ps[:, SAMPLE:TOK], ona_hi[:, f, SAMPLE:TOK].bitcast(F32),
                                  ALU.subtract).then_inc(on_lo, 1)
            with dve.Fori(0, NK) as j:
                for a in range(4):
                    dve.wait_ge(ada2_hid, j * 4 + (a + 1))
                    dve.tensor_tensor(ada_rest_lo[:, a], ada_rest[:, a], ada_rest_hi[:, a % 2].bitcast(F32), ALU.subtract)\
                       .then_inc(ada2_lod, 1)
                dve.wait_ge(mixlo_set, j)
                dve.wait_ge(bg_ps, j + 1)
                dve.tensor_tensor(by_half(t1[:, :]), halves(PJ, 1),
                                  by_half(sg[:, bass.ds(j, 1), :].rearrange("p a n -> p (a n)")), ALU.mult).then_inc(t1_set, 1)
                dve.wait_ge(ada2_used, j * 4 + 4)
                dve.wait_ge(ada2_ps, j)
                dve.tensor_copy(rest_rows[0:4, :], PA[0:4, 1024:1536]).then_inc(ada2_rows, 1)
                dve.wait_ge(bn_ps, j + 1)
                dve.wait_ge(sn_set, j + 1)
                dve.tensor_tensor(by_half(t2[:, :]), halves(PA, 0), by_half(sn[:, :]), ALU.mult).then_inc(t2_set, 1)
                dve.wait_ge(t1_set, j + 1)
                dve.wait_ge(t2_set, j + 1)
                dve.tensor_tensor(t1[:, :], t1[:, :], t2[:, :], ALU.add).then_inc(mixf_set, 1)
                dve.wait_ge(mixhi_set, j + 1)
                dve.tensor_tensor(mix_lo[:, bass.ds(j, 1), :], t1[:, :].unsqueeze(1),
                                  mix_hi[:, bass.ds(j, 1), :].bitcast(F32), ALU.subtract).then_inc(mixlo_set, 1)
                dve.wait_ge(ada2_ps, j + 1)
                dve.tensor_tensor(mod[:, bass.ds(j * 4 + ADA_FIRST, 4), :], PA[:, 1536:1544].rearrange("p (a c) -> p a c", c=2),
                                  bc(vec[:, 0, bass.ds(j * 4 + (V_BADA + ADA_FIRST), 4)].unsqueeze(2), [P, 4, 2]), ALU.add)\
                   .then_inc(ada2_cp, 1)
            dve.wait_ge(ada2_cp, NK)
            dve.tensor_scalar(a2[:, :, :], mod[:, 4 * NK:5 * NK, :], 1.0, None, ALU.add).then_inc(mod_all, 1)
            dve.wait_ge(mod_all, 1)
            dve.tensor_tensor(a2[:, :, :], a2[:, :, :], bc(vec[:, 0, V_GFFN:V_GFFN + NK].unsqueeze(2), [P, NK, 2]),
                              ALU.mult).then_inc(mod_all, 1)
            dve.wait_ge(mod_all, 2)
            dve.memset(zeros[:, :], 0.0).then_inc(zero_set, 1)
            dve.memset(x2_sq[:, 1, :], 0.0).then_inc(zero_set, 1)

            def pieces(pair):
                o = pair * 2 * BANK
                return ((slice(0, HALF), PJ[:, o:o + HALF], 0),
                        (slice(HALF, SAMPLE), PJ[:, o + BANK:o + BANK + SAMPLE - HALF], 0),
                        (slice(SAMPLE, TOK), PJ[:, o + BANK + SAMPLE - HALF:o + BANK + HALF], 1))

            with dve.Fori(0, 4) as i:
                for b in range(2):
                    dve.wait_ge(xc_cp, i * 2 + (b + 1))
                    dve.wait_ge(out_ps, i * 2 + (b + 1))
                    for cols, ps, req in pieces(b):
                        x_ = x2[:, bass.ds(i * 2 + b, 1), cols]
                        ins = dve.scalar_tensor_tensor(
                            out=x_, in0=ps.unsqueeze(1),
                            scalar=mod[:, bass.ds(i * 2 + (2 * NK + b), 1), req:req + 1].rearrange("p a b -> p (a b)"),
                            in1=x_, op0=ALU.mult, op1=ALU.add)
                    ins.then_inc(x2_set, 1)
            dve.wait_ge(rs2_done, 1)
            modulated(x2, rstd2, h2_t, h2_f, a2, lambda k, r: mod[:, 3 * NK + k, r:r + 1], h2t_set, h2f_set, h2hi_set, h2lo_set)
            dve.wait_ge(h2lo_set, NK)
            dve.memset(ua[:, :], 0.0).then_inc(pad_set, 1)
            dve.memset(ug[:, :], 0.0).then_inc(pad_set, 1)
            n = TOK + 1

            def tap(s, col):
                return vec[:, s, bass.ds(col, 1)]

            with dve.Fori(0, NF) as j:
                dve.wait_ge(actlo_set, j)
                for u, o, first, step, done in ((ua, ca, 0, ca_step, ua_set), (ug, cg, NF, cg_step, ug_set)):
                    dve.wait_ge(done, j + 1)
                    dve.tensor_scalar(o[:, :], u[:, 1:1 + n], tap(1, j + (V_W1 + first)), tap(2, j + first), ALU.mult, ALU.add)\
                       .then_inc(step, 1)
                    dve.wait_ge(step, j * 3 + 1)
                    dve.scalar_tensor_tensor(out=o[:, :], in0=u[:, 0:n], scalar=tap(0, j + (V_W0 + first)), in1=o[:, :],
                                             op0=ALU.mult, op1=ALU.add).then_inc(step, 1)
                    dve.wait_ge(step, j * 3 + 2)
                    dve.scalar_tensor_tensor(out=o[:, :], in0=u[:, 2:2 + n], scalar=tap(1, j + (V_W2 + first)), in1=o[:, :],
                                             op0=ALU.mult, op1=ALU.add).then_inc(step, 1)
                dve.wait_ge(silu_set, j + 1)
                dve.wait_ge(ca_step, j * 3 + 3)
                dve.tensor_tensor(ca[:, :], ca[:, :], cg[:, :], ALU.mult).then_inc(prod_set, 1)
                dve.wait_ge(prod_set, j + 1)
                dve.wait_ge(acthi_set, j + 1)
                jt = bass.ds(j, 1)
                dve.tensor_tensor(act_lo[:, jt, 0:SAMPLE], ca[:, 0:SAMPLE].unsqueeze(1),
                                  act_hi[:, jt, 0:SAMPLE].bitcast(F32), ALU.subtract)
                dve.tensor_tensor(act_lo[:, jt, SAMPLE:TOK], ca[:, SAMPLE + 1:n].unsqueeze(1),
                                  act_hi[:, jt, SAMPLE:TOK].bitcast(F32), ALU.subtract).then_inc(actlo_set, 1)
            with dve.Fori(0, 4) as i:
                for b in range(2):
                    dve.wait_ge(dn_ps, i * 6 + (3 * b + 3))
                    dve.wait_ge(yt_ps, i * 2)
                    for cols, ps, req in pieces(b):
                        ins = dve.scalar_tensor_tensor(
                            out=yT[:, b:b + 1, cols], in0=ps.unsqueeze(1),
                            scalar=mod[:, bass.ds(i * 2 + (5 * NK + b), 1), req:req + 1].rearrange("p a b -> p (a b)"),
                            in1=x2[:, bass.ds(i * 2 + b, 1), cols], op0=ALU.mult, op1=ALU.add)
                    ins.then_inc(y_set, 1)


_INS = ["x_prompt", "x_sample", "c", "cache_na_k", "cache_na_v", "state_gla_fwd", "state_gla_bwd", "c_ctx", "w_ada",
        "b_ada", "g_norm_mix", "w_in", "w_alpha_fwd", "b_alpha_fwd", "w_alpha_bwd", "b_alpha_bwd", "g_gla_norm",
        "g_q_norm", "g_k_norm", "rpb", "w_gla_o", "w_na_o", "w_out", "g_norm_ffn", "w_up", "w_conv", "b_conv", "w_down"]
_OUTS = [(1, CONTEXT, D), (1, SAMPLE, D), (1, 1, CONTEXT, NH, HD), (1, 1, CONTEXT, NH, HD),
         (1, 1, GH, DK, DV), (1, 1, GH, DK, DV)]


def constant_tables():
    import numpy as np

    p = np.arange(P)
    tables = np.zeros((P, 384 + 896 + 2), np.float32)
    tables[:, 0:128] = np.eye(P)
    tables[:, 128:256] = 1
    tables[:, 256:384] = p[:, None] // HD == p[None, :] // HD
    tables[:, 1280:1282] = p[:, None] % 2 == np.arange(2)[None, :]
    col = p % GC
    for at_, first, group, offsets in ((384, 1, None, (-1, 0, 1)), (768, 0, 0, (0, 1)), (1024, 3, 3, (-1, 0))):
        for n, o in enumerate(offsets):
            q = first * GC + col[:, None]
            k = (first + o) * GC + col[None, :]
            start = np.clip(q - WC // 2, 0, GRID_W - WC)
            tables[:, at_ + n * P:at_ + (n + 1) * P] = np.where((k >= start) & (k < start + WC), 0, MASKED)
    masks = np.zeros((P, N_LEVEL, P), np.uint8)
    masks[:, 0, :] = np.eye(P)
    for n in range(1, N_LEVEL):
        w = 64 >> (n - 1)
        b = p // w
        masks[:, n, :] = (b[:, None] // 2 == b[None, :] // 2) & (b[:, None] != b[None, :])
    return tables, masks.view(np.int32)


def kernel(**inputs):
    import numpy as _np
    import concourse.bacc as _bacc
    from concourse import mybir as _mybir
    from concourse.bass_utils import run_bass_kernel_spmd as _run

    nc = _bacc.Bacc("TRN2", target_bir_lowering=False, num_devices=1)
    arrays, args = {}, []

    def add(name, a):
        arrays[f"in_{name}_dram"] = a
        args.append(nc.dram_tensor(f"in_{name}_dram", a.shape, _mybir.dt.from_np(a.dtype), kind="ExternalInput").ap())

    for name in _INS:
        add(name, _np.ascontiguousarray(inputs[name]))
    for name, table in zip(("tables", "level_masks"), constant_tables()):
        add(name, table)
    for i, shape in enumerate(_OUTS):
        args.append(nc.dram_tensor(f"out_{i}_dram", shape, F32, kind="ExternalOutput").ap())
    hybrid_dit_step(nc, *args)
    r = _run(nc, [arrays], core_ids=[0])
    return tuple(r.results[0][f"out_{i}_dram"] for i in range(len(_OUTS)))
```

```python
from contextlib import ExitStack

import concourse.bass as bass
from concourse import mybir

P = 128
F32 = mybir.dt.float32
F32R = mybir.dt.float32r
U8 = mybir.dt.uint8
I32 = mybir.dt.int32
ACT = mybir.ActivationFunctionType
ALU = mybir.AluOpType

D = 1024
NK = D // P
SAMPLE, CONTEXT = 512, 128
TOK = SAMPLE + CONTEXT
NT = TOK // P
HALF = TOK // 2
BANK = 512
PAST = 256
GH, DK, DV = 4, 64, 128
NH, HD = 8, 64
GRID_W, ROWS = 64, 8
GC = 16
WR, WC = 8, 16
D_FF = 2816
NF = D_FF // P
EPS = 1e-6
MASKED = -8e30
IN_Z = 1536
IN_NA, IN_MGLA, IN_MNA = 1568, 3104, 4128

C_Z = 0
C_GLA = C_Z + 1
C_NA = C_GLA + 12
C_MG = C_NA + 12
C_POST = C_MG + 8
C_OUT = C_POST + 16
C_UP = C_OUT + 8
C_DOWN = C_UP + 2 * NF
DOWN_K = [8, 7, 7]

ADA_FIRST = 16
ADA_SLOTS = 6
ADA_HI = 4
ADA_LAG = 2

V_W0, V_BADA, V_GMIX, V_GFFN, V_BAF, V_BAB, V_GGLA, V_GQ, V_GK = 0, 44, 92, 100, 108, 110, 112, 113, 114
V_W1, V_W2, V_C, V_CCTX = 0, 44, 88, 96
ROWS_0, ROWS_1, ROWS_2 = 115, 104, 44

KEYS = [(0, 2, 384), (0, 3, 0), (1, 3, 0), (2, 2, 640)]
GATE_K = [(0, 0, 2), (0, 2, 2), (0, 4, 2), (0, 6, 1), (0, 7, 1),
          (1, 0, 1), (1, 1, 1), (1, 2, 1), (1, 3, 1), (1, 4, 2), (1, 6, 2)]
N_LEVEL = 8


def hybrid_dit_step(nc, x_prompt, x_sample, c, cache_k, cache_v, state_f, state_b, c_ctx, w_ada, b_ada,
                    g_mix, w_in, w_af, b_af, w_ab, b_ab, g_gla, g_q, g_k, rpb, w_gla_o, w_na_o, w_out,
                    g_ffn, w_up, w_conv, b_conv, w_down, tables, level_masks,
                    y_prompt, y_sample, new_k, new_v, new_sf, new_sb):
    with ExitStack() as ctx:
        base = 16512

        def at(name, offset, shape, dt=F32):
            return nc.alloc_sbuf_tensor_at(name, [P] + list(shape), dt, offset=base + offset)

        def sem(name):
            return ctx.enter_context(nc.semaphore(name))

        ident = at("ident", 0, [P])
        ones = at("ones", 512, [P])
        blk64 = at("blk64", 1024, [P])
        vec = at("vec", 1536, [3, P])
        mod = at("mod", 3072, [48, 2])
        a1 = at("a1", 3456, [NK, 2])
        a2 = at("a2", 3456, [NK, 2])
        cond4 = at("cond4", 3520, [NK, 4], F32R)
        eps = at("eps", 3648, [1])
        one = at("one", 3680, [1])
        pick = vec[:, 2, ROWS_2:ROWS_2 + 2]
        RAW = 3712
        wraw = at("wraw", RAW, [2, 8, P])
        whi = at("whi", RAW + 8192, [2, 8, P], F32R)
        wlo = at("wlo", RAW + 16384, [2, 8, P], F32R)
        H = RAW + 24576
        h_hi = at("h_hi", H, [NK, TOK], F32R)
        h_lo = at("h_lo", H + 20480, [NK, TOK], F32R)
        R = H + 40960
        x_rows = at("x_rows", R + 25600, [NT, D])
        ada_first = at("ada_first", R + 46080, [ADA_SLOTS, 2, 4 * P])
        ada_lo = at("ada_lo", R + 46080, [ADA_SLOTS, 2, 4 * P], F32R)
        ada_hi = at("ada_hi", H, [ADA_HI, 2, 4 * P], F32R)
        mod_rows = at("mod_rows", H + 20480, [4, 4 * P])
        xT = at("xT", R + 107616, [NK, TOK])
        x_sq = at("x_sq", R + 87136, [2, TOK])
        rstd = at("rstd", R + 92256, [TOK])
        h_t = at("h_t", R + 94816, [2, TOK])
        cond_sig = at("cond_sig", R + 102496, [2 * NK])
        cond = at("cond", R + 102560, [2, NK])
        rpb_rows = at("rpb_rows", R + 0, [NH, ROWS, 31])
        rpb_wide = at("rpb_wide", R + 128096, [NH, ROWS, 48])
        vec_rows = at("vec_rows", R + 104000, [3, P])
        kc_tok = at("kc_tok", R + 76800, [2, NH * HD])
        window = at("window", R + 0, [896])
        level_mask = at("level_mask", R + 3584, [N_LEVEL, P], U8)
        bias8 = at("bias8", R + 5120, [NH, 384])
        kcT = at("kcT", R + 17408, [4, PAST])
        vc = at("vc", R + 21504, [2, NH * HD])
        nqk = at("nqk", R + 25600, [8, TOK])
        nv_tok = at("nv_tok", R + 46080, [NT, NH * HD])
        v_tok = at("v_tok", R + 56320, [NT, GH * DV])
        lvl = at("lvl", R + 66560, [2, 4, TOK])
        la_e = at("la_e", R + 66560, [4, TOK])
        la_m = at("la_m", R + 76800, [4, TOK])
        Y = at("Y", R + 87040, [4, NT, P + 1])
        U = at("U", R + 97376, [12, TOK])
        A = at("A", R + 107616, [2, NT, 2, P])
        kt = at("kt", R + 97376, [2, NT, 256])
        S = at("S", R + 87040, [2, 4, 2, DV])
        nvraw = at("nvraw", R + 128096, [4, TOK])
        oT = at("oT", R + 97376, [GH, TOK])
        z = at("z", R + 138336, [TOK])
        w_alpha = at("w_alpha", R + 140896, [4 * P])
        decay = at("decay", R + 138336, [4, NT])
        s_out = at("s_out", R + 140896, [2, 2, DV])
        og_sq = at("og_sq", R + 107616, [2, TOK])
        og_rs = at("og_rs", R + 112736, [2, TOK])
        og_hi = at("og_hi", R + 66560, [GH, TOK], F32R)
        og_lo = at("og_lo", R + 76800, [GH, TOK], F32R)
        sg = at("sg", R + 107616, [NK, TOK])
        o_tok = at("o_tok", R + 128096, [NT, NH * HD])
        qk_rs = [at(f"qk_rs{n}", o, [2, TOK]) for n, o in enumerate((R + 56320, R + 61440, R + 128096, R + 133216))]
        qk_n = at("qk_n", R + 61440, [2, TOK])
        kc_pair = at("kc_pair", R + 87040, [PAST])
        k_out = at("k_out", R + 138496, [NH * HD])
        bias = at("bias", R + 88064, [2, 896])
        sc = at("sc", R + 95232, [2, TOK])
        pT = at("pT", R + 100352, [2, TOK])
        mx = at("mx", R + 105984, [2, 10])
        nmx = at("nmx", R + 106080, [10])
        psm = at("psm", R + 106144, [10])
        rin = at("rin", R + 106208, [10])
        ona_hi = at("ona_hi", R + 87040, [4, TOK], F32R)
        ona_lo = at("ona_lo", R + 97280, [4, TOK], F32R)
        mix_hi = at("mix_hi", R + 0, [NK, TOK], F32R)
        mix_lo = at("mix_lo", R + 20480, [NK, TOK], F32R)
        ada_rest = at("ada_rest", R + 40960, [4, 2, 4 * P])
        ada_rest_lo = at("ada_rest_lo", R + 40960, [4, 2, 4 * P], F32R)
        ada_rest_hi = at("ada_rest_hi", R + 128096, [2, 2, 4 * P], F32R)
        rest_rows = at("rest_rows", R + 136288, [4 * P])
        sn = at("sn", R + 57344, [TOK])
        t1 = at("t1", R + 59904, [TOK])
        t2 = at("t2", R + 62464, [TOK])
        x_cols = at("x_cols", R + 57344, [2, NT, P])
        x2_sq = at("x2_sq", R + 62464, [2, TOK])
        zeros = at("zeros", R + 67584, [HALF])
        x2 = at("x2", R + 123008, [NK, TOK])
        rstd2 = at("rstd2", R + 0, [TOK])
        h2_t = at("h2_t", R + 2560, [2, TOK])
        ua = at("ua", R + 0, [TOK + 3])
        ug = at("ug", R + 2592, [TOK + 3])
        ca = at("ca", R + 5184, [TOK + 1])
        cg = at("cg", R + 7776, [TOK + 1])
        act_hi = at("act_hi", R + 10368, [NF, TOK], F32R)
        act_lo = at("act_lo", R + 66688, [NF, TOK], F32R)
        yT = at("yT", R + 0, [2, TOK])
        y_tok = at("y_tok", R + 5120, [2, NT, P])

        PJ = ctx.enter_context(nc.psum_tensor("PJ", [P, 4 * BANK], F32))
        PA = ctx.enter_context(nc.psum_tensor("PA", [P, 4 * BANK], F32))

        def halves(ps, pair):
            return ps[:, pair * 2 * BANK:(pair + 1) * 2 * BANK].rearrange("p (b n) -> p b n", b=2)[:, :, 0:HALF]

        def by_half(t):
            return t.rearrange("p (b n) -> p b n", b=2)

        tab_in = sem("tab_in")
        ones_in, x_in = sem("ones_in"), sem("x_in")
        cvec_in, vec_in = sem("cvec_in"), sem("vec_in")
        past_in, mask_in = sem("past_in"), sem("mask_in")
        rpb_in, rpb_moved = sem("rpb_in"), sem("rpb_moved")
        ada_in = [sem(f"ada_in{i}") for i in range(ADA_SLOTS)]
        ada_hid, ada_lod, ada_used = sem("ada_hid"), sem("ada_lod"), sem("ada_used")
        raw_in = [sem("raw_in0"), sem("raw_in1")]
        hi_done, lo_done, slot_freed = sem("hi_done"), sem("lo_done"), sem("slot_freed")
        const_set = sem("const_set")
        vec_ps, vec_done = sem("vec_ps"), sem("vec_done")
        cond_sg, cond_done, cvec_done = sem("cond_sg"), sem("cond_done"), sem("cvec_done")
        xt_ps, xt_cp, xt_sq, xt_st = sem("xt_ps"), sem("xt_cp"), sem("xt_sq"), sem("xt_st")
        kct_ps, kct_cp = sem("kct_ps"), sem("kct_cp")
        rows_set, mod_ps, mod_set, a1_set = sem("rows_set"), sem("mod_ps"), sem("mod_set"), sem("a1_set")
        rs_ln, rs_done = sem("rs_ln"), sem("rs_done")
        ht_set, hhi_set, hlo_set = sem("ht_set"), sem("hhi_set"), sem("hlo_set")
        bias8_set = sem("bias8_set")
        tile_ready, tile_freed = sem("tile_ready"), sem("tile_freed")
        la_ps, la_abs, la_exp, la_ln, la_min, la_sub, la_sum = (sem(n) for n in (
            "la_ps", "la_abs", "la_exp", "la_ln", "la_min", "la_sub", "la_sum"))
        q_scaled = sem("q_scaled")
        vt_ps = sem("vt_ps")
        lv_arg, lv_exp, lv_set, lv_ps, lv_cp = (sem(n) for n in (
            "lv_arg", "lv_exp", "lv_set", "lv_ps", "lv_cp"))
        kt_ps = sem("kt_ps")
        decay_set, s0_in, kv_ps, s_set, s_copied, s_stored = (sem(n) for n in (
            "decay_set", "s0_in", "kv_ps", "s_set", "s_copied", "s_stored"))
        gr_silu, o_ps, o_cp = sem("gr_silu"), sem("o_ps"), sem("o_cp")
        og_sqd, og_st, og_ln, og_rsd, og_n, og_g, og_hid, og_lod = (sem(n) for n in (
            "og_sqd", "og_st", "og_ln", "og_rsd", "og_n", "og_g", "og_hid", "og_lod"))
        nvt_ps, nvt_cp, nv_stored = sem("nvt_ps"), sem("nvt_cp"), sem("nv_stored")
        bias_set, sq_set, sq_ps, sq_ln, sq_rs, nqk_set, qk_set, kcp_set, ko_ps, ko_cp, ko_stored = (sem(n) for n in (
            "bias_set", "sq_set", "sq_ps", "sq_ln", "sq_rs", "nqk_set", "qk_set", "kcp_set", "ko_ps", "ko_cp", "ko_stored"))
        sc_ps, sc_mx, sc_cp, sc_exp, pt_ps, pt_cp, pv_ps, rin_set, pv_cp, gate_cp = (sem(n) for n in (
            "sc_ps", "sc_mx", "sc_cp", "sc_exp", "pt_ps", "pt_cp", "pv_ps", "rin_set", "pv_cp", "gate_cp"))
        on_ps, on_hi, on_lo = sem("on_ps"), sem("on_hi"), sem("on_lo")
        mna_ps, bg_ps, bn_ps, sg_set, sn_set, t1_set, t2_set, mixf_set, mixhi_set, mixlo_set = (sem(n) for n in (
            "mna_ps", "bg_ps", "bn_ps", "sg_set", "sn_set", "t1_set", "t2_set", "mixf_set", "mixhi_set", "mixlo_set"))
        ada2_in = [sem(f"ada2_in{i}") for i in range(4)]
        ada2_hid, ada2_lod, ada2_used, ada2_rows, ada2_ps, ada2_cp, mod_all = (sem(n) for n in (
            "ada2_hid", "ada2_lod", "ada2_used", "ada2_rows", "ada2_ps", "ada2_cp", "mod_all"))
        xc_in = [sem("xc_in0"), sem("xc_in1")]
        out_ps, xc_ps, xc_cp, x2_set, x2_sqd, x2_st, zero_set = (sem(n) for n in (
            "out_ps", "xc_ps", "xc_cp", "x2_set", "x2_sqd", "x2_st", "zero_set"))
        rs2_ln, rs2_done, h2t_set, h2hi_set, h2lo_set, pad_set = (sem(n) for n in (
            "rs2_ln", "rs2_done", "h2t_set", "h2hi_set", "h2lo_set", "pad_set"))
        up_ps, ua_set, ug_set, ca_step, cg_step, silu_set, prod_set, acthi_set, actlo_set = (sem(n) for n in (
            "up_ps", "ua_set", "ug_set", "ca_step", "cg_step", "silu_set", "prod_set", "acthi_set", "actlo_set"))
        dn_ps, y_set, yt_ps, y_cp = (sem(n) for n in ("dn_ps", "y_set", "yt_ps", "y_cp"))
        y_stored = [sem("y_stored0"), sem("y_stored1")]

        w_in_v = w_in[0].rearrange("(k p) n -> p k n", p=P)
        w_ada_v = w_ada[0].rearrange("(k p) n -> p k n", p=P)
        w_go_v = w_gla_o[0].rearrange("(k p) n -> p k n", p=P)
        w_no_v = w_na_o[0].rearrange("(k p) n -> p k n", p=P)
        w_out_v = w_out[0].rearrange("(k p) n -> p k n", p=P)
        w_up_v = w_up[0].rearrange("(k p) n -> p k n", p=P)
        w_dn_v = w_down[0].rearrange("(k p) n -> p k n", p=P)
        xs_v = x_sample[0].rearrange("(t p) d -> p t d", p=P)
        ys_v = y_sample[0].rearrange("(t p) d -> p t d", p=P)

        block = ctx.enter_context(nc.Block())

        @block.sync
        def _(sp):
            def chunk(slot, n, src, col, free, k=8, src2=None):
                if free is not None:
                    sp.wait_ge(lo_done, free)
                    sp.sem_inc(slot_freed, 1)
                if src2 is None:
                    sp.dma_start(wraw[:, slot, 0:4, :], src[:, n:n + 4, bass.ds(col, P)]).then_inc(raw_in[slot], 16)
                    sp.dma_start(wraw[:, slot, 4:k, :], src[:, n + 4:n + k, bass.ds(col, P)]).then_inc(raw_in[slot], 16)
                else:
                    sp.dma_start(wraw[:, slot, 0:4, :], src[:, 0:4, bass.ds(col, P)]).then_inc(raw_in[slot], 16)
                    sp.dma_start(wraw[:, slot, 4:8, :], src2[:, 0:4, bass.ds(col, P)]).then_inc(raw_in[slot], 16)

            def ada_piece(at_, q):
                return w_ada_v[:, 2 * q:2 * q + 2, at_:at_ + 4 * P] if isinstance(at_, int) else \
                    w_ada_v[:, 2 * q:2 * q + 2, bass.ds(at_, 4 * P)]

            sp.dma_start(ident[:, :], tables[:, 0:128]).then_inc(tab_in, 16)
            sp.dma_start(x_rows[:, 0:NT - 1, :], xs_v).then_inc(x_in, 16)
            sp.dma_start(x_rows[:, NT - 1, :], x_prompt[0]).then_inc(x_in, 16)
            sp.dma_start(ones[:, :], tables[:, 128:256]).then_inc(ones_in, 16)
            sp.dma_start(blk64[:, :], tables[:, 256:384]).then_inc(ones_in, 16)
            for a in range(ADA_FIRST):
                if a >= ADA_SLOTS:
                    sp.wait_ge(ada_used, a - ADA_SLOTS + 1)
                sp.dma_start(ada_first[:, a % ADA_SLOTS, :, :], ada_piece(a // 4 * 4 * P, a % 4))\
                  .then_inc(ada_in[a % ADA_SLOTS], 16)
                if a == 12:
                    chunk(0, 0, w_in_v, IN_Z, None)
                    chunk(1, 0, w_in_v, 0, None)
            with sp.Fori(0, 5) as i:
                chunk(0, 0, w_in_v, i * 256 + 128, i * 2 + 1)
                chunk(1, 0, w_in_v, i * 256 + 256, i * 2 + 2)
            chunk(0, 0, w_in_v, 11 * P, 11)
            with sp.Fori(0, 10) as i:
                chunk(1, 0, w_in_v, i * 256 + IN_NA, i * 2 + C_NA - 1)
                chunk(0, 0, w_in_v, i * 256 + (IN_NA + 128), i * 2 + C_NA)
            chunk(1, 0, w_in_v, IN_MNA, C_POST - 1)
            chunk(0, 0, w_go_v, 0, C_POST, src2=w_no_v)
            sp.wait_ge(nvt_cp, NT)
            sp.wait_ge(pv_cp, 40)
            sp.wait_ge(nv_stored, 16)

            def ada_rest_piece(a, at_):
                sp.dma_start(ada_rest[:, a, :, :], ada_piece(at_, a)).then_inc(ada2_in[a], 16)

            for a in range(4):
                ada_rest_piece(a, ADA_FIRST * P)
            with sp.Fori(0, NK - 1) as j:
                chunk(1, 0, w_in_v, j * 128 + (IN_MNA + P), j * 2 + (C_POST + 1))
                sp.wait_ge(ada2_used, j * 4 + 2)
                sp.sem_inc(slot_freed, 1)
                for a in (0, 1):
                    ada_rest_piece(a, j * 512 + (ADA_FIRST + 4) * P)
                chunk(0, 0, w_go_v, j * 128 + P, j * 2 + (C_POST + 2), src2=w_no_v)
                sp.wait_ge(ada2_used, j * 4 + 4)
                sp.sem_inc(slot_freed, 1)
                for a in (2, 3):
                    ada_rest_piece(a, j * 512 + (ADA_FIRST + 4) * P)
            with sp.Fori(0, 4) as i:
                for b in range(2):
                    chunk((b + 1) % 2, 0, w_out_v, i * 256 + b * 128, i * 2 + (C_OUT - 1 + b))
                sp.wait_ge(mixlo_set, NK)
                sp.wait_ge(xc_ps, i * 2)
                sp.sem_inc(slot_freed, 1)
                for b in range(2):
                    sp.dma_start(x_cols[:, b, 0:4, :], xs_v[:, :, bass.ds(i * 256 + b * 128, P)]).then_inc(xc_in[b], 16)
                    sp.dma_start(x_cols[:, b, 4, :], x_prompt[0][:, bass.ds(i * 256 + b * 128, P)]).then_inc(xc_in[b], 16)
            with sp.Fori(0, NF) as j:
                chunk(1, 0, w_up_v, j * 128, j * 2 + C_UP - 1)
                chunk(0, 0, w_up_v, j * 128 + D_FF, j * 2 + C_UP)
            with sp.Fori(0, 4) as i:
                for b in range(2):
                    for q in range(3):
                        n = 3 * b + q
                        chunk((n + 1) % 2, sum(DOWN_K[:q]), w_dn_v, i * 256 + b * 128, i * 6 + (C_DOWN - 1 + n), k=DOWN_K[q])

        @block.gpsimd
        def _(pool):
            def lo(slot, ready, k=8):
                pool.wait_ge(hi_done, ready)
                pool.tensor_tensor(wlo[:, slot, 0:k, :], wraw[:, slot, 0:k, :],
                                   whi[:, slot, 0:k, :].bitcast(F32), ALU.subtract).then_inc(lo_done, 1)

            pool.dma_start(kc_tok[:, :, :], cache_k[0, 0].rearrange("(b p) h d -> p b (h d)", p=P)).then_inc(past_in, 16)
            pool.dma_start(vc[:, :, :], cache_v[0, 0].rearrange("(b p) h d -> p b (h d)", p=P)).then_inc(past_in, 16)
            for q in range(ROWS):
                src = rpb[0, :, ROWS - 1 - q:2 * ROWS - 1 - q, :].unsqueeze(0).to_broadcast([GC, NH, ROWS, 31])
                pool.dma_start(rpb_rows[q * GC:(q + 1) * GC, :, :, :], src).then_inc(rpb_in, 16)
            pool.wait_ge(const_set, 4)
            pool.dma_start(w_alpha[0:16, 0:256], w_af[0]).then_inc(past_in, 16)
            pool.dma_start(w_alpha[16:32, 256:512], w_ab[0]).then_inc(past_in, 16)
            pool.wait_ge(rpb_in, 16 * ROWS)
            for q in range(GC):
                pool.dma_start(rpb_wide[q:q + 7 * GC + 1:GC, :, :, q + 1:q + 32], rpb_rows[q:q + 7 * GC + 1:GC, :, :, :])\
                    .then_inc(rpb_moved, 16)
            lo(0, 1)
            lo(1, 2)
            pool.wait_ge(rpb_moved, 16 * GC)
            for o in range(3):
                ins = pool.tensor_scalar(bias8[:, :, o * P:(o + 1) * P].rearrange("p h (r c) -> p h r c", c=GC),
                                         rpb_wide[:, :, :, o * GC:(o + 1) * GC], 8.0, None, ALU.mult)
            ins.then_inc(bias8_set, 1)
            with pool.Fori(0, 5) as i:
                lo(0, i * 2 + 3)
                lo(1, i * 2 + 4)
            lo(0, 13)
            with pool.Fori(0, 6) as i:
                lo(1, i * 2 + C_NA + 1)
                lo(0, i * 2 + C_NA + 2)
            pool.wait_ge(tile_freed, C_NA + 8)
            pool.wait_ge(o_ps, 6)
            for n in range(4):
                if n == 2:
                    pool.wait_ge(nvt_ps, NT)
                for x in range(2):
                    pool.tensor_tensor(qk_rs[n][:, x, :], nqk[:, n + 4 * x, :], nqk[:, n + 4 * x, :], ALU.mult)\
                        .then_inc(sq_set, 1)
            pool.wait_ge(bias8_set, 1)
            pool.wait_ge(mask_in, 32)
            pool.wait_ge(o_ps, 6)
            with pool.Fori(0, 4) as j:
                pool.wait_ge(sc_cp, j * 10)
                b8 = bias8[:, bass.ds(j * 2, 2), :]
                for lo_at, n, src in ((0, 384, 0), (384, 256, 128), (640, 256, 0)):
                    mk = window[:, lo_at:lo_at + n].unsqueeze(1).to_broadcast([P, 2, n])
                    pool.tensor_tensor(bias[:, :, lo_at:lo_at + n], b8[:, :, src:src + n], mk, ALU.add)\
                        .then_inc(bias_set, 1)
                lo(1, j * 2 + C_MG + 1)
                lo(0, j * 2 + C_MG + 2)
            with pool.Fori(0, NK) as j:
                lo(1, j * 2 + C_POST + 1)
                lo(0, j * 2 + C_POST + 2)
            with pool.Fori(0, 4) as j:
                lo(1, j * 2 + C_OUT + 1)
                lo(0, j * 2 + C_OUT + 2)
            with pool.Fori(0, NF) as j:
                lo(1, j * 2 + C_UP + 1)
                lo(0, j * 2 + C_UP + 2)
            with pool.Fori(0, 4) as i:
                for n in range(6):
                    lo((n + 1) % 2, i * 6 + C_DOWN + 1 + n)

        @block.tensor
        def _(pe):
            def project(slot, ready, hi, lo, ps, pair, k0=0, k1=8, w0=0, start=True, stop=True, done=None):
                if ready is not None:
                    pe.wait_ge(lo_done, ready)
                for k in range(k0, k1):
                    for b in range(2):
                        out = ps[:, (2 * pair + b) * BANK:(2 * pair + b) * BANK + HALF]
                        tok = slice(b * HALF, (b + 1) * HALF)
                        pe.matmul(out, whi[:, slot, w0 + k, :], hi(k)[:, tok], start=start and k == k0, stop=False)
                        pe.matmul(out, whi[:, slot, w0 + k, :], lo(k)[:, tok], start=False, stop=False)
                    for b in range(2):
                        out = ps[:, (2 * pair + b) * BANK:(2 * pair + b) * BANK + HALF]
                        tok = slice(b * HALF, (b + 1) * HALF)
                        mm = pe.matmul(out, wlo[:, slot, w0 + k, :], hi(k)[:, tok], start=False, stop=stop and k == k1 - 1)
                if done is not None:
                    mm.then_inc(done, 1)

            hh = lambda k: h_hi[:, k, :]
            hl = lambda k: h_lo[:, k, :]

            pe.wait_ge(tab_in, 32)
            pe.wait_ge(cvec_in, 16 * 3)
            pe.transpose(PA[:, 1024:1024 + ROWS_1], vec_rows[0:ROWS_1, 1, :], ident[0:ROWS_1, 0:ROWS_1]).then_inc(vec_ps, 1)
            pe.wait_ge(x_in, 32)
            pe.wait_ge(ones_in, 32)

            def x_stats(f):
                pe.wait_ge(xt_sq, f + 1)
                for b in range(2):
                    mm = pe.matmul(PJ[:, b * BANK:b * BANK + HALF], ones[:, :], x_sq[:, f % 2, b * HALF:(b + 1) * HALF],
                                   start=f == 0, stop=f == NK - 1)
                mm.then_inc(xt_st, 1)

            def modulation(out, w_hi, w_lo, q):
                for k in range(2):
                    pe.matmul(out, cond4[:, 2 * q + k, :], w_hi[:, k, :], start=q == 0 and k == 0, stop=False)
                    mm = pe.matmul(out, cond4[:, 2 * q + k, :], w_lo[:, k, :], start=False, stop=q == 3 and k == 1)
                return mm

            def rows_to_columns(g):
                pe.wait_ge(rows_set, g + 1)
                for a in range(4 * g, 4 * g + 4):
                    mm = pe.matmul(PA[:, 1536 + 2 * a:1536 + 2 * a + 2], mod_rows[0:4, g, a % 4 * P:(a % 4 + 1) * P],
                                   pick[0:4, :], start=True, stop=True)
                mm.then_inc(mod_ps, 1)

            for f in range(NK + ADA_LAG + 1):
                if f == NK + 1:
                    pe.wait_ge(xt_cp, NK)
                    rows_to_columns(0)
                    rows_to_columns(1)
                if f < NK:
                    if f == 1:
                        pe.wait_ge(cvec_done, 1)
                    if f >= 2:
                        pe.wait_ge(xt_cp, f - 1)
                    for t in range(NT):
                        tr = pe.transpose(PA[:, (f % 2) * 1024 + t * P:(f % 2) * 1024 + (t + 1) * P],
                                          x_rows[:, t, f * P:(f + 1) * P], ident[:, :])
                    tr.then_inc(xt_ps, 1)
                if 1 <= f <= NK:
                    x_stats(f - 1)
                if f > ADA_LAG:
                    if f == ADA_LAG + 1:
                        pe.wait_ge(cond_done, 3)
                    for a in (2 * (f - ADA_LAG) - 2, 2 * (f - ADA_LAG) - 1):
                        pe.wait_ge(ada_lod, a + 1)
                        if a % 4 == 0 and a >= 8:
                            pe.wait_ge(rows_set, a // 4 - 1)
                        bank_ = (2 + a // 4 % 2) * BANK
                        modulation(PJ[0:4, bank_:bank_ + BANK], ada_hi[:, a % ADA_HI], ada_lo[:, a % ADA_SLOTS], a % 4)\
                            .then_inc(ada_used, 1)
            pe.wait_ge(vec_in, 16 * 12)
            pe.wait_ge(xt_cp, NK)
            for s, n in ((0, ROWS_0), (2, ROWS_2)):
                pe.transpose(PA[:, 1024 + s * P:1024 + s * P + n], vec_rows[0:n, s, :], ident[0:n, 0:n]).then_inc(vec_ps, 1)
            rows_to_columns(2)
            rows_to_columns(3)
            pe.wait_ge(past_in, 64)
            for j in range(4):
                for b in range(2):
                    tr = pe.transpose(PA[:, j * PAST + b * P:j * PAST + (b + 1) * P], kc_tok[:, b, j * P:(j + 1) * P], ident[:, :])
            tr.then_inc(kct_ps, 1)

            pe.wait_ge(lo_done, 2)
            for k in range(NK + 4):
                if k < NK:
                    pe.wait_ge(hlo_set, k + 1)
                    project(0, None, hh, hl, PJ, 0, k0=k, k1=k + 1, start=k == 0, stop=k == NK - 1,
                            done=tile_ready if k == NK - 1 else None)
                if k >= 4:
                    project(1, None, hh, hl, PJ, 1, k0=k - 4, k1=k - 3, start=k == 4, stop=k == NK + 3,
                            done=tile_ready if k == NK + 3 else None)
            pe.wait_ge(tile_freed, 1)
            pe.wait_ge(kct_cp, 1)
            pe.wait_ge(vec_done, 1)
            for m in range(4):
                if m >= 2:
                    pe.wait_ge(la_abs, m - 1)
                    pe.wait_ge(la_min, m - 1)
                for b in range(2):
                    mm = pe.matmul(PA[:, (m % 2) * 1024 + b * BANK:(m % 2) * 1024 + b * BANK + HALF],
                                   w_alpha[0:32, m * P:(m + 1) * P], z[0:32, b * HALF:(b + 1) * HALF], start=True, stop=True)
                mm.then_inc(la_ps, 1)
            with pe.Fori(0, 5) as i:
                for b in range(2):
                    pe.wait_ge(tile_freed, i * 2 + (b + 1))
                    project(b, i * 2 + (b + 3), hh, hl, PJ, b, done=tile_ready)
            pe.wait_ge(tile_freed, 11)
            project(0, 13, hh, hl, PJ, 0, done=tile_ready)
            bank_seq = [0]

            def next_bank():
                n = bank_seq[0]
                bank_seq[0] += 1
                if n >= 4:
                    pe.wait_ge(lv_cp, n - 3)
                return (n % 4) * BANK

            def v_rows():
                pe.wait_ge(tile_freed, 9)
                pe.wait_ge(la_abs, 4)
                pe.wait_ge(la_min, 4)
                for t in range(NT):
                    at_ = next_bank()
                    for f in range(4):
                        tr = pe.transpose(PA[:, at_ + f * P:at_ + (f + 1) * P], U[:, 4 + f, t * P:(t + 1) * P], ident[:, :])
                    tr.then_inc(vt_ps, 1)

            def level(n):
                w = n % 2
                pe.wait_ge(lv_set, n + 1)
                for r in range(2):
                    for t0 in (0, 2, 4):
                        at_ = next_bank()
                        for t in range(t0, min(t0 + 2, NT)):
                            for dt in range(2):
                                o = at_ + ((t - t0) * 2 + dt) * P
                                mm = pe.matmul(PA[:, o:o + P], lvl[64 * r:64 * r + 64, w, 2 + dt, t * P:(t + 1) * P],
                                               lvl[64 * r:64 * r + 64, w, dt, t * P:(t + 1) * P], start=True, stop=True)
                        mm.then_inc(lv_ps, 1)

            def key_rows():
                for d in range(2):
                    pe.wait_ge(lv_set, N_LEVEL + d + 1)
                    for t0 in (0, 2, 4):
                        at_ = next_bank()
                        for t in range(t0, min(t0 + 2, NT)):
                            for dt in range(2):
                                o = at_ + ((t - t0) * 2 + dt) * P
                                tr = pe.transpose(PA[:, o:o + P], lvl[:, d, 2 + dt, t * P:(t + 1) * P], ident[:, :])
                        tr.then_inc(kt_ps, 1)

            def attention_tile(a):
                n = C_NA + a
                pe.wait_ge(tile_freed, n - 1)
                project(n % 2, n + 1, hh, hl, PJ, n % 2, done=tile_ready)

            for a in range(11):
                attention_tile(a)
                if a == 0:
                    v_rows()
                elif a <= N_LEVEL:
                    level(a - 1)
                elif a == 10:
                    key_rows()
            base_cp = bank_seq[0]
            pe.wait_ge(lv_cp, base_cp)
            for s in range(4):
                for d in range(2):
                    t = NT - 1 if s == 3 else (s if d == 0 else 3 - s)
                    for hd in range(GH):
                        dt, r = hd // 2, hd % 2
                        o = s * BANK + d * 256 + dt * P
                        mm = pe.matmul(PA[64 * r:64 * r + 64, o:o + P],
                                       kt[:, d, t, dt * P + 64 * r:dt * P + 64 * r + 64],
                                       v_tok[:, t, hd * DV:(hd + 1) * DV], start=True, stop=True)
                mm.then_inc(kv_ps, 1)
            attention_tile(11)
            pe.wait_ge(s_set, 12)
            pe.wait_ge(s_copied, 1)
            g = 0
            for r in range(2):
                for t0 in (0, 2, 4):
                    if g >= 4:
                        pe.wait_ge(o_cp, g - 3)
                    for t in range(t0, min(t0 + 2, NT)):
                        for dt in range(2):
                            hd = 2 * dt + r
                            o = (g % 4) * BANK + ((t - t0) * 2 + dt) * P
                            mm = pe.matmul(PA[:, o:o + P], v_tok[:, t, hd * DV:(hd + 1) * DV], A[:, r, t, dt, :],
                                           start=True, stop=t == NT - 1)
                            if t < NT - 1:
                                for d in range(2):
                                    mm = pe.matmul(PA[:, o:o + P], S[64 * r:64 * r + 64, d, t, dt, :],
                                                   lvl[64 * r:64 * r + 64, d, dt, t * P:(t + 1) * P],
                                                   start=False, stop=d == 1)
                    mm.then_inc(o_ps, 1)
                    g += 1
            pe.wait_ge(tile_freed, C_NA + 12)
            for t in range(NT):
                pe.wait_ge(o_cp, (5, 6, 6, 6, 6)[t])
                if t == 4:
                    pe.wait_ge(nvt_cp, 1)
                for f in range(4):
                    tr = pe.transpose(PA[:, (t % 4) * BANK + f * P:(t % 4) * BANK + (f + 1) * P],
                                      nvraw[:, f, t * P:(t + 1) * P], ident[:, :])
                tr.then_inc(nvt_ps, 1)
            for n in range(4):
                pe.wait_ge(og_sqd, n + 1)
                if n >= 2:
                    pe.wait_ge(og_ln, n - 1)
                for b in range(2):
                    mm = pe.matmul(PJ[:, (n % 2) * 1024 + b * BANK:(n % 2) * 1024 + b * BANK + HALF], ones[:, :],
                                   og_sq[:, n % 2, b * HALF:(b + 1) * HALF], start=True, stop=True)
                mm.then_inc(og_st, 1)
                pe.wait_ge(sq_set, n * 2 + 2)
                if n == 0:
                    pe.wait_ge(nvt_cp, NT)
                else:
                    pe.wait_ge(sq_ln, n)
                for x in range(2):
                    for b in range(2):
                        mm = pe.matmul(PA[:, (2 * x + b) * BANK:(2 * x + b) * BANK + HALF], blk64[:, :],
                                       qk_rs[n][:, x, b * HALF:(b + 1) * HALF], start=True, stop=True)
                mm.then_inc(sq_ps, 1)
            pe.wait_ge(og_ln, 4)
            pe.wait_ge(sq_ln, 4)

            for f in range(4):
                pe.wait_ge(nqk_set, 2 * f + 2)
                tr = pe.transpose(PA[:, 1024 + f * P:1024 + (f + 1) * P], nqk[:, 4 + f, SAMPLE:TOK], ident[:, :])
            tr.then_inc(ko_ps, 1)

            with pe.Fori(0, 4) as j:
                pe.wait_ge(qk_set, j + 1)
                for m in range(11):
                    if m < 10:
                        r, i = m // 5, m % 5
                        hs = slice(64 * r, 64 * r + 64)
                        pe.wait_ge(sc_cp, j * 10 + m)
                        q = qk_n[hs, 0, i * P:(i + 1) * P]
                        if i < 4:
                            t0, nt, _ = KEYS[i]
                            pe.matmul(PA[:, 0:nt * P], q, qk_n[hs, 1, t0 * P:(t0 + nt) * P], start=True, stop=True)
                            pe.wait_ge(pv_cp, j * 10 + max(m - 2, 0))
                            if m == 0:
                                pe.wait_ge(kcp_set, j + 1)
                            pe.matmul(PA[:, BANK:BANK + PAST], q, kc_pair[hs, :], start=True, stop=True).then_inc(sc_ps, 1)
                        else:
                            pe.matmul(PA[:, 0:P], q, qk_n[hs, 1, SAMPLE:TOK], start=True, stop=True).then_inc(sc_ps, 1)
                    if m >= 1:
                        i = (m - 1) % 5
                        nb = KEYS[i][1] + 2 if i < 4 else 1
                        pe.wait_ge(sc_exp, j * 10 + m)
                        if m >= 2:
                            pe.wait_ge(pt_cp, j * 10 + (m - 1))
                        else:
                            pe.wait_ge(ko_cp, 1)
                        for b in range(nb):
                            tr = pe.transpose(PA[:, 1024 + b * P:1024 + (b + 1) * P],
                                              sc[:, (m - 1) % 2, b * P:(b + 1) * P], ident[:, :])
                        tr.then_inc(pt_ps, 1)
                    b, k, nk = GATE_K[m]
                    if m == 5:
                        pe.wait_ge(gate_cp, j * 2)
                    if m == 9:
                        pe.wait_ge(gate_cp, j * 2 + 1)
                    project((b + 1) % 2, j * 2 + (C_MG + b + 1) if k == 0 else None, hh, hl, PJ, (b + 1) % 2,
                            k0=k, k1=k + nk, start=k == 0, stop=k + nk == 8, done=tile_ready if k + nk == 8 else None)
                    if m >= 1:
                        r, i = (m - 1) // 5, (m - 1) % 5
                        pe.wait_ge(pt_cp, j * 10 + m)
                        if m >= 2:
                            pe.wait_ge(pv_cp, j * 10 + (m - 1))
                        else:
                            pe.wait_ge(sc_cp, j * 10 + (m + 1))
                        o = BANK + 256 + 64 * ((m - 1) % 2)
                        col = j * 128 + r * 64
                        if i < 4:
                            t0, nt, _ = KEYS[i]
                            vs = [nv_tok[:, t0 + b, bass.ds(col, HD)] for b in range(nt)] + \
                                 [vc[:, b, bass.ds(col, HD)] for b in range(2)]
                        else:
                            vs = [nv_tok[:, 4, bass.ds(col, HD)]]
                        for b, v in enumerate(vs):
                            mm = pe.matmul(PA[:, o:o + HD], pT[:, (m - 1) % 2, b * P:(b + 1) * P], v,
                                           start=b == 0, stop=b == len(vs) - 1)
                        mm.then_inc(pv_ps, 1)
            pe.wait_ge(pv_cp, 40)
            for f in range(4):
                if f >= 2:
                    pe.wait_ge(on_lo, f - 1)
                for t in range(NT):
                    tr = pe.transpose(PA[:, (f % 2) * 1024 + t * P:(f % 2) * 1024 + (t + 1) * P],
                                      o_tok[:, t, f * P:(f + 1) * P], ident[:, :])
                tr.then_inc(on_ps, 1)
            pe.wait_ge(on_lo, 4)
            pe.wait_ge(og_lod, 4)
            pe.wait_ge(gate_cp, NK)
            def rest(j, pieces_):
                for a in pieces_:
                    pe.wait_ge(ada2_lod, j * 4 + (a + 1))
                    modulation(PA[0:4, 1024:1536], ada_rest_hi[:, a % 2], ada_rest_lo[:, a], a).then_inc(ada2_used, 1)

            with pe.Fori(0, NK) as j:
                pe.wait_ge(sn_set, j)
                project(1, j * 2 + C_POST + 1, hh, hl, PJ, 0, done=mna_ps)
                rest(j, (0, 1))
                pe.wait_ge(t1_set, j)
                project(0, j * 2 + C_POST + 2, lambda k: og_hi[:, k, :], lambda k: og_lo[:, k, :], PJ, 1, k1=4, done=bg_ps)
                rest(j, (2, 3))
                pe.wait_ge(t2_set, j)
                project(0, None, lambda k: ona_hi[:, k, :], lambda k: ona_lo[:, k, :], PA, 0, k1=4, w0=4, done=bn_ps)
                pe.wait_ge(ada2_rows, j + 1)
                pe.wait_ge(ada2_cp, j)
                for a in range(4):
                    mm = pe.matmul(PA[:, 1536 + 2 * a:1536 + 2 * a + 2], rest_rows[0:4, a * P:(a + 1) * P], pick[0:4, :],
                                   start=True, stop=True)
                mm.then_inc(ada2_ps, 1)
            pe.wait_ge(mixlo_set, NK)
            pe.wait_ge(ada2_cp, NK)
            pe.wait_ge(zero_set, 2)
            for b in range(2):
                pe.matmul(PA[:, (2 + b) * BANK:(2 + b) * BANK + HALF], ones[:, :], zeros[:, :], start=True, stop=False)

            def x2_stats(slot, stop):
                for b in range(2):
                    mm = pe.matmul(PA[:, (2 + b) * BANK:(2 + b) * BANK + HALF], ones[:, :],
                                   x2_sq[:, slot, b * HALF:(b + 1) * HALF], start=False, stop=stop)
                mm.then_inc(x2_st, 1)

            mh = lambda k: mix_hi[:, k, :]
            ml = lambda k: mix_lo[:, k, :]
            with pe.Fori(0, 4) as i:
                for b in range(2):
                    project((b + 1) % 2, i * 2 + (C_OUT + b + 1), mh, ml, PJ, b, done=out_ps)
                    pe.wait_ge(xc_in[b], i * 32 + 32)
                    pe.wait_ge(xc_cp, i * 2 + b)
                    for t in range(NT):
                        tr = pe.transpose(PA[:, t * P:(t + 1) * P], x_cols[:, b, t, :], ident[:, :])
                    tr.then_inc(xc_ps, 1)
                    pe.wait_ge(x2_sqd, i * 2 + b)
                    x2_stats((b + 1) % 2, False)
            pe.wait_ge(x2_sqd, NK)
            x2_stats(1, True)

            pe.wait_ge(x2_set, NK)
            pe.wait_ge(lo_done, C_UP + 2)
            for k in range(NK + 4):
                if k < NK:
                    pe.wait_ge(h2lo_set, k + 1)
                    project(1, None, hh, hl, PJ, 0, k0=k, k1=k + 1, start=k == 0, stop=k == NK - 1,
                            done=up_ps if k == NK - 1 else None)
                if k >= 4:
                    project(0, None, hh, hl, PJ, 1, k0=k - 4, k1=k - 3, start=k == 4, stop=k == NK + 3,
                            done=up_ps if k == NK + 3 else None)
            with pe.Fori(0, NF - 1) as j:
                pe.wait_ge(ua_set, j + 1)
                project(1, j * 2 + (C_UP + 3), hh, hl, PJ, 0, done=up_ps)
                pe.wait_ge(ug_set, j + 1)
                project(0, j * 2 + (C_UP + 4), hh, hl, PJ, 1, done=up_ps)
            def out_rows(b, done, copied):
                pe.wait_ge(y_set, done)
                if copied is not None:
                    pe.wait_ge(y_cp, copied)
                for t in range(NT):
                    tr = pe.transpose(PA[:, b * 1024 + t * P:b * 1024 + (t + 1) * P], yT[:, b, t * P:(t + 1) * P], ident[:, :])
                tr.then_inc(yt_ps, 1)

            def down_step(i, first):
                for b in range(2):
                    k0 = 0
                    if not first:
                        pe.wait_ge(y_set, i * 2 + (b - 1))
                    for q in range(3):
                        n = 3 * b + q
                        if q == 2:
                            pe.wait_ge(actlo_set, NF)
                        project((n + 1) % 2, i * 6 + (C_DOWN + n + 1), lambda k, k0=k0: act_hi[:, k0 + k, :],
                                lambda k, k0=k0: act_lo[:, k0 + k, :], PJ, b, k1=DOWN_K[q],
                                start=q == 0, stop=q == 2, done=dn_ps)
                        k0 += DOWN_K[q]
                        if n == 3:
                            out_rows(0, i * 2 + 1, None if first else i * 2 - 1)
                        if n == 0 and not first:
                            out_rows(1, i * 2, i * 2 - 2)

            pe.wait_ge(ua_set, NF)
            pe.wait_ge(ug_set, NF)
            pe.wait_ge(actlo_set, NF - 1)
            down_step(0, True)
            with pe.Fori(0, 3) as i:
                down_step(i + 1, False)
            out_rows(1, 8, 6)

        def level_view(x, w):
            return lvl[:, x[0], 2 * x[1]:2 * x[1] + 2, :].rearrange("p d (t a b c) -> p (d t a) b c", t=NT, b=2, c=w)

        def y_view(d):
            return Y[:, 2 * d:2 * d + 2, :, :].rearrange("p d t n -> p (d t) n")

        @block.scalar
        def _(act):
            def on_constant():
                act.wait_ge(const_set, 4)

            def hi(slot, loaded):
                act.wait_ge(raw_in[slot], loaded * 32)
                act.activation(whi[:, slot, :, :], wraw[:, slot, :, :], ACT.Copy).then_inc(hi_done, 1)

            def shifted(k, t_set, t, shift, hi_set):
                act.wait_ge(t_set, k + 1)
                act.activation(h_hi[:, k, 0:SAMPLE], t[:, k % 2, 0:SAMPLE], ACT.Identity, bias=shift[:, 0:1])
                act.activation(h_hi[:, k, SAMPLE:TOK], t[:, k % 2, SAMPLE:TOK], ACT.Identity, bias=shift[:, 1:2]).then_inc(hi_set, 1)

            conv = w_conv[0].rearrange("t (r n) -> t r n", n=P)
            act.dma_start(vec_rows[V_C:V_C + 8, 1, :], c[0].rearrange("(r n) -> r n", n=P)).then_inc(cvec_in, 16)
            act.dma_start(vec_rows[V_CCTX:V_CCTX + 8, 1, :], c_ctx.rearrange("(r n) -> r n", n=P)).then_inc(cvec_in, 16)
            act.dma_start(pick[0:4, :], tables[0:4, 1280:1282]).then_inc(tab_in, 16)
            act.dma_start(vec_rows[0:88, 1, :], conv[1:3].rearrange("t r n -> (t r) n")).then_inc(cvec_in, 16)
            for v, at_, n in ((w_conv[0, 0], V_W0, 44), (b_ada[0], V_BADA, 48), (g_mix[0], V_GMIX, 8), (g_ffn[0], V_GFFN, 8),
                              (b_af[0], V_BAF, 2), (b_ab[0], V_BAB, 2), (g_gla[0], V_GGLA, 1)):
                act.dma_start(vec_rows[at_:at_ + n, 0, :], v.rearrange("(r n) -> r n", n=P)).then_inc(vec_in, 16)
            act.dma_start(vec_rows[0:44, 2, :], b_conv[0].rearrange("(r n) -> r n", n=P)).then_inc(vec_in, 16)
            for v, at_, o in ((g_q[0], V_GQ, 0), (g_k[0], V_GK, 0), (g_q[0], V_GQ, 64), (g_k[0], V_GK, 64)):
                act.dma_start(vec_rows[at_:at_ + 1, 0, o:o + HD], v.rearrange("(r n) -> r n", n=HD)).then_inc(vec_in, 16)
            act.wait_ge(cvec_done, 1)
            act.activation(cond_sig[:, :], vec[:, 1, V_C:V_C + 16], ACT.Sigmoid).then_inc(cond_sg, 1)
            act.preload_act_table_set("natural_log_exp_and_others")
            act.wait_ge(const_set, 4)
            for f in range(NK + ADA_LAG):
                if f >= ADA_LAG:
                    for a in (2 * (f - ADA_LAG), 2 * (f - ADA_LAG) + 1):
                        act.wait_ge(ada_in[a % ADA_SLOTS], 16 * (a // ADA_SLOTS + 1))
                        if a >= ADA_HI:
                            act.wait_ge(ada_used, a - ADA_HI + 1)
                        act.activation(ada_hi[:, a % ADA_HI], ada_first[:, a % ADA_SLOTS], ACT.Copy).then_inc(ada_hid, 1)
                if f < NK:
                    act.wait_ge(xt_cp, f + 1)
                    if f >= 2:
                        act.wait_ge(xt_st, f - 1)
                    act.activation(x_sq[:, f % 2, :], xT[:, f, :], ACT.Square).then_inc(xt_sq, 1)
            hi(0, 1)
            hi(1, 1)
            act.wait_ge(xt_st, NK)
            act.activation(by_half(rstd[:, :]), halves(PJ, 0), ACT.Ln, bias=eps[:, :], scale=1.0 / D).then_inc(rs_ln, 1)
            act.wait_ge(rs_ln, 1)
            act.activation(rstd[:, :], rstd[:, :], ACT.Exp, scale=-0.5).then_inc(rs_done, 1)
            act.wait_ge(kct_ps, 1)
            act.activation(kcT[:, :, :].rearrange("p a b -> p (a b)"), PA[:, 0:1024], ACT.Copy).then_inc(kct_cp, 1)
            act.wait_ge(rpb_moved, 16 * GC)
            act.dma_start(window[:, :], tables[:, 384:384 + 896]).then_inc(mask_in, 16)
            act.dma_start(level_mask[:, :, :].bitcast(I32), level_masks).then_inc(mask_in, 16)
            for k in range(NK):
                shifted(k, ht_set, h_t, mod[:, k, :], hhi_set)
            act.wait_ge(bias8_set, 1)
            act.wait_ge(tile_ready, 1)
            hi(0, 2)
            act.activation(by_half(z[0:32, :]), halves(PJ, 0)[0:32], ACT.Copy).then_inc(tile_freed, 1)
            for m in range(4):
                act.wait_ge(la_ps, m + 1)
                act.activation(by_half(la_e[:, m, :]), halves(PA, m % 2), ACT.Abs,
                               bias=vec[:, 0, V_BAF + m:V_BAF + m + 1]).then_inc(la_abs, 1)
                act.wait_ge(la_abs, m + 1)
                act.activation(la_e[:, m, :], la_e[:, m, :], ACT.Exp, scale=-1.0).then_inc(la_exp, 1)
                act.wait_ge(la_exp, m + 1)
                act.activation(la_e[:, m, :], la_e[:, m, :], ACT.Ln, bias=one[:, :]).then_inc(la_ln, 1)
            with act.Fori(0, 6) as i:
                for b in range(2):
                    act.wait_ge(tile_ready, i * 2 + (b + 2))
                    hi((b + 1) % 2, i + (2 + b))
                    act.activation(by_half(U[:, bass.ds(i * 2 + b, 1), :].rearrange("p a n -> p (a n)")),
                                   halves(PJ, (b + 1) % 2), ACT.Copy).then_inc(tile_freed, 1)
            act.wait_ge(tile_freed, 13)
            act.activation(U[:, 8:12, :], U[:, 8:12, :], ACT.Silu).then_inc(gr_silu, 1)
            act.preload_act_table_set("natural_log_exp_and_others")
            for a in range(12):
                n = C_NA + a
                act.wait_ge(tile_ready, n + 1)
                hi(n % 2, (n + 2) // 2 + 1)
                dst = nqk[:, a, :] if a < 8 else nvraw[:, a - 8, :]
                grouped = dst[:, 0:SAMPLE].rearrange("p (g r c) -> p r g c", g=4, c=GC)
                ps = halves(PJ, n % 2)
                act.activation(grouped[:, 0:5], ps[:, 0, :].rearrange("p (r g c) -> p r g c", g=4, c=GC), ACT.Copy)
                act.activation(grouped[:, 5:8], ps[:, 1, 0:192].rearrange("p (r g c) -> p r g c", g=4, c=GC), ACT.Copy)
                act.activation(dst[:, SAMPLE:TOK], ps[:, 1, 192:HALF], ACT.Copy).then_inc(tile_freed, 1)
                if a < 9:
                    lv = a + 1
                    act.wait_ge(lv_arg, lv)
                    act.activation(lvl[:, lv % 2, :, :], lvl[:, lv % 2, :, :], ACT.Exp, scale=1.0 / 16).then_inc(lv_exp, 1)
                if a == 10:
                    act.wait_ge(decay_set, 1)
                    for d, st in enumerate((state_f, state_b)):
                        act.dma_start(S[:, d, 3 * d, :, :], st[0, 0].rearrange("(t r) d v -> (r d) t v", r=2)).then_inc(s0_in, 16)
                if a == 9:
                    act.activation(decay[:, :, :], Y[:, :, :, P:P + 1].rearrange("p m t o -> p m (t o)"), ACT.Exp,
                                   scale=1.0 / 16).then_inc(decay_set, 1)
            act.wait_ge(s_copied, 1)
            for d, st in enumerate((new_sf, new_sb)):
                act.dma_start(st[0, 0].rearrange("(t r) d v -> (r d) t v", r=2), s_out[:, d, :, :]).then_inc(s_stored, 16)
            g = 0
            o_v = oT[:, :, :].rearrange("p (dt r) (t n) -> p r t dt n", r=2, n=P)
            for r in range(2):
                for t0 in (0, 2, 4):
                    nt = min(2, NT - t0)
                    act.wait_ge(o_ps, g + 1)
                    act.activation(o_v[:, r, t0:t0 + nt], PA[:, (g % 4) * BANK:(g % 4) * BANK + nt * 256]
                                   .rearrange("p (t dt n) -> p t dt n", dt=2, n=P), ACT.Copy).then_inc(o_cp, 1)
                    g += 1
            act.wait_ge(o_cp, 6)

            def gla_square(hd):
                act.activation(og_sq[:, hd % 2, :], oT[:, hd, :], ACT.Square).then_inc(og_sqd, 1)

            def gla_hi(hd):
                act.wait_ge(og_g, hd + 1)
                act.activation(og_hi[:, hd, :], oT[:, hd, :], ACT.Copy).then_inc(og_hid, 1)

            gla_square(0)
            gla_square(1)
            for n in range(4):
                act.wait_ge(og_st, n + 1)
                if n >= 2:
                    act.wait_ge(og_n, n - 1)
                act.activation(by_half(og_rs[:, n % 2, :]), halves(PJ, n % 2), ACT.Ln, bias=eps[:, :],
                               scale=1.0 / DV).then_inc(og_ln, 1)
                act.wait_ge(sq_ps, n + 1)
                qk = qk_rs[n][:, :, :]
                act.activation(qk.rearrange("p x (b n) -> p (x b) n", b=2),
                               PA[:, :].rearrange("p (b n) -> p b n", b=4)[:, :, 0:HALF], ACT.Ln,
                               bias=eps[:, :], scale=1.0 / HD).then_inc(sq_ln, 1)
                act.wait_ge(og_ln, n + 1)
                act.activation(og_rs[:, n % 2, :], og_rs[:, n % 2, :], ACT.Exp, scale=-0.5).then_inc(og_rsd, 1)
                act.wait_ge(sq_ln, n + 1)
                act.activation(qk, qk, ACT.Exp, scale=-0.5).then_inc(sq_rs, 1)
                if n + 2 < 4:
                    gla_square(n + 2)
                if n >= 1:
                    gla_hi(n - 1)
            gla_hi(GH - 1)
            act.dma_start(new_v[0, 0].rearrange("s h d -> s (h d)"), nv_tok[:, NT - 1, :]).then_inc(nv_stored, 16)
            act.wait_ge(og_lod, GH)
            act.wait_ge(ko_ps, 1)
            act.activation(k_out[:, :], PA[:, 1024:1024 + NH * HD], ACT.Copy).then_inc(ko_cp, 1)
            act.wait_ge(ko_cp, 1)
            act.dma_start(new_k[0, 0].rearrange("s h d -> s (h d)"), k_out[:, :]).then_inc(ko_stored, 16)
            act.activation(kc_pair[:, :], kcT[:, 0, :], ACT.Copy).then_inc(kcp_set, 1)

            with act.Fori(0, 4) as j:
                on_constant()
                for m in range(11):
                    if m >= 1:
                        i = (m - 1) % 5
                        n = (KEYS[i][1] + 2) * P if i < 4 else P
                        act.wait_ge(pt_ps, j * 10 + m)
                        if m >= 3:
                            act.wait_ge(pv_ps, j * 10 + (m - 2))
                        act.activation(pT[:, (m - 1) % 2, 0:n], PA[:, 1024:1024 + n], ACT.Copy).then_inc(pt_cp, 1)
                    if m == 10:
                        act.activation(kc_pair[:, :].unsqueeze(1), kcT[:, bass.ds((j + 1) % 4, 1), :], ACT.Copy)\
                           .then_inc(kcp_set, 1)
                    if m < 10:
                        i = m % 5
                        n = (KEYS[i][1] + 2) * P if i < 4 else P
                        act.wait_ge(sc_cp, j * 10 + (m + 1))
                        act.activation(sc[:, m % 2, 0:n], sc[:, m % 2, 0:n], ACT.Exp, bias=nmx[:, m:m + 1],
                                       accum_out=psm[:, m:m + 1]).then_inc(sc_exp, 1)
                    if m in (5, 10):
                        b = m // 5 - 1
                        act.wait_ge(tile_ready, j * 2 + (C_MG + b + 1))
                        hi((b + 1) % 2, j + (14 + b))
                        act.activation(by_half(sg[:, bass.ds(j * 2 + b, 1), :].rearrange("p a n -> p (a n)")),
                                       halves(PJ, (b + 1) % 2), ACT.Copy).then_inc(gate_cp, 1)
            act.wait_ge(kcp_set, 5)
            for f in range(4):
                act.wait_ge(on_ps, f + 1)
                ps = PA[:, (f % 2) * 1024:(f % 2) * 1024 + TOK]
                act.activation(ona_hi[:, f, 0:SAMPLE].rearrange("p (r g c) -> p r g c", g=4, c=GC),
                               ps[:, 0:SAMPLE].rearrange("p (g r c) -> p r g c", g=4, c=GC), ACT.Copy)
                act.activation(ona_hi[:, f, SAMPLE:TOK], ps[:, SAMPLE:TOK], ACT.Copy).then_inc(on_hi, 1)
            def rest_hi(j, a):
                act.wait_ge(ada2_in[a], j * 16 + 16)
                act.wait_ge(ada2_used, j * 4 + max(a - 1, 0))
                act.activation(ada_rest_hi[:, a % 2], ada_rest[:, a], ACT.Copy).then_inc(ada2_hid, 1)

            act.preload_act_table_set("sigmoid_and_others")
            with act.Fori(0, NK) as j:
                on_constant()
                act.wait_ge(gate_cp, NK)
                act.activation(sg[:, bass.ds(j, 1), :], sg[:, bass.ds(j, 1), :], ACT.Sigmoid).then_inc(sg_set, 1)
                rest_hi(j, 0)
                rest_hi(j, 1)
                act.wait_ge(mna_ps, j + 1)
                hi(1, j + 18)
                act.wait_ge(t2_set, j)
                act.activation(by_half(sn[:, :]), halves(PJ, 0), ACT.Sigmoid).then_inc(sn_set, 1)
                rest_hi(j, 2)
                rest_hi(j, 3)
                act.wait_ge(bn_ps, j + 1)
                hi(0, j + 19)
                on_constant()
                act.wait_ge(mixf_set, j + 1)
                act.activation(mix_hi[:, bass.ds(j, 1), :], t1[:, :].unsqueeze(1), ACT.Copy).then_inc(mixhi_set, 1)
            act.wait_ge(ko_stored, 16)
            act.preload_act_table_set("natural_log")
            with act.Fori(0, 4) as i:
                for b in range(2):
                    act.wait_ge(out_ps, i * 2 + (b + 1))
                    hi((b + 1) % 2, i + (26 + b))
                    on_constant()
                    act.wait_ge(xc_ps, i * 2 + (b + 1))
                    act.activation(x2[:, bass.ds(i * 2 + b, 1), :], PA[:, 0:TOK].unsqueeze(1), ACT.Copy).then_inc(xc_cp, 1)
                    on_constant()
                    act.wait_ge(x2_set, i * 2 + (b + 1))
                    act.wait_ge(x2_st, i * 2 + b)
                    act.activation(x2_sq[:, b:b + 1, :], x2[:, bass.ds(i * 2 + b, 1), :], ACT.Square).then_inc(x2_sqd, 1)
            act.wait_ge(x2_st, NK + 1)
            act.activation(by_half(rstd2[:, :]), halves(PA, 1), ACT.Ln, bias=eps[:, :], scale=1.0 / D).then_inc(rs2_ln, 1)
            act.wait_ge(rs2_ln, 1)
            act.activation(rstd2[:, :], rstd2[:, :], ACT.Exp, scale=-0.5).then_inc(rs2_done, 1)
            for k in range(NK):
                shifted(k, h2t_set, h2_t, mod[:, 3 * NK + k, :], h2hi_set)
            act.preload_act_table_set("silu_and_others")
            act.wait_ge(pad_set, 2)
            with act.Fori(0, NF) as j:
                for b, (u, step, done) in enumerate(((ua, ca_step, ua_set), (ug, cg_step, ug_set))):
                    act.wait_ge(up_ps, j * 2 + (b + 1))
                    hi((b + 1) % 2, j + (30 + b))
                    act.wait_ge(step, j * 3)
                    ps = halves(PJ, b)
                    act.activation(u[:, 1:1 + HALF], ps[:, 0, :], ACT.Copy)
                    act.activation(u[:, 1 + HALF:1 + SAMPLE], ps[:, 1, 0:SAMPLE - HALF], ACT.Copy)
                    act.activation(u[:, 2 + SAMPLE:2 + TOK], ps[:, 1, SAMPLE - HALF:HALF], ACT.Copy).then_inc(done, 1)
                act.wait_ge(cg_step, j * 3 + 3)
                act.activation(cg[:, :], cg[:, :], ACT.Silu).then_inc(silu_set, 1)
                on_constant()
                act.wait_ge(prod_set, j + 1)
                act.activation(act_hi[:, bass.ds(j, 1), 0:SAMPLE], ca[:, 0:SAMPLE].unsqueeze(1), ACT.Copy)
                act.activation(act_hi[:, bass.ds(j, 1), SAMPLE:TOK], ca[:, SAMPLE + 1:TOK + 1].unsqueeze(1), ACT.Copy)\
                   .then_inc(acthi_set, 1)

            def rows_out(b, n, stored):
                act.wait_ge(yt_ps, n)
                if stored is not None:
                    act.wait_ge(y_stored[b], stored)
                act.activation(y_tok[:, b, :, :].rearrange("p t n -> p (t n)"), PA[:, b * 1024:b * 1024 + TOK],
                               ACT.Copy).then_inc(y_cp, 1)
                act.wait_ge(y_cp, n)
                col = (n - 1) * P
                act.dma_start(ys_v[:, :, cols(col)], y_tok[:, b, 0:4, :]).then_inc(y_stored[b], 16)
                act.dma_start(y_prompt[0][:, cols(col)], y_tok[:, b, 4, :]).then_inc(y_stored[b], 16)

            def cols(col):
                return slice(col, col + P) if isinstance(col, int) else bass.ds(col, P)

            def down(i, first, last):
                for n in range(6):
                    act.wait_ge(dn_ps, i * 6 + (n + 1))
                    if not (last and n >= 4):
                        hi((n + 1) % 2, i * 3 + ((C_DOWN + 2 + n) // 2 + 1))
                    if n == 0 and not first:
                        rows_out(1, i * 2, i * 32 - 32)
                    if n == 3:
                        rows_out(0, i * 2 + 1, None if first else i * 32)

            down(0, True, False)
            with act.Fori(0, 2) as i:
                down(i + 1, False, False)
            down(3, False, True)
            rows_out(1, 8, 96)
            for b in range(2):
                act.wait_ge(y_stored[b], 4 * 32)
            act.wait_ge(s_stored, 2 * 16)
            act.wait_ge(nv_stored, 16)

        @block.vector
        def _(dve):
            def bc(ap, shape):
                return ap.to_broadcast(shape)

            def on_constant():
                dve.wait_ge(const_set, 4)

            dve.memset(eps[:, :], EPS).then_inc(const_set, 1)
            dve.memset(one[:, :], 1.0).then_inc(const_set, 1)
            dve.memset(w_alpha[:, :], 0.0).then_inc(const_set, 1)
            dve.memset(rpb_wide[:, :, :, :], 0.0).then_inc(const_set, 1)
            dve.wait_ge(vec_ps, 1)
            dve.tensor_copy(vec[:, 1, 0:ROWS_1], PA[:, 1024:1024 + ROWS_1]).then_inc(cvec_done, 1)
            dve.wait_ge(cvec_done, 1)
            dve.wait_ge(cond_sg, 1)
            dve.tensor_tensor(cond[:, :, :].rearrange("p a b -> p (a b)"), vec[:, 1, V_C:V_C + 16], cond_sig[:, :],
                              ALU.mult).then_inc(cond_done, 1)
            dve.wait_ge(cond_done, 1)
            by_vector = cond[:, :, :].rearrange("p a k -> p k a")
            dve.tensor_copy(cond4[:, :, 0:2], by_vector).then_inc(cond_done, 1)
            dve.wait_ge(cond_done, 2)
            dve.tensor_tensor(cond4[:, :, 2:4], by_vector, cond4[:, :, 0:2].bitcast(F32), ALU.subtract).then_inc(cond_done, 1)

            def rows_out(g):
                dve.wait_ge(ada_used, 4 * g + 4)
                dve.tensor_copy(mod_rows[0:4, g, :], PJ[0:4, (2 + g % 2) * BANK:(3 + g % 2) * BANK]).then_inc(rows_set, 1)

            for f in range(NK + ADA_LAG):
                if f < NK:
                    dve.wait_ge(xt_ps, f + 1)
                    dve.tensor_copy(xT[:, f, :], PA[:, (f % 2) * 1024:(f % 2) * 1024 + TOK]).then_inc(xt_cp, 1)
                if f >= ADA_LAG:
                    for a in (2 * (f - ADA_LAG), 2 * (f - ADA_LAG) + 1):
                        dve.wait_ge(ada_hid, a + 1)
                        dve.tensor_tensor(ada_lo[:, a % ADA_SLOTS], ada_first[:, a % ADA_SLOTS],
                                          ada_hi[:, a % ADA_HI].bitcast(F32), ALU.subtract).then_inc(ada_lod, 1)
                    if f - ADA_LAG >= 3 and (f - ADA_LAG) % 2 == 1:
                        rows_out((f - ADA_LAG - 3) // 2)
            rows_out(3)
            dve.wait_ge(vec_ps, 3)
            dve.tensor_copy(vec[:, 0, 0:ROWS_0], PA[:, 1024:1024 + ROWS_0])
            dve.tensor_copy(vec[:, 2, 0:ROWS_2], PA[:, 1024 + 2 * P:1024 + 2 * P + ROWS_2]).then_inc(vec_done, 1)
            dve.wait_ge(vec_done, 1)
            dve.wait_ge(mod_ps, 4)
            dve.tensor_tensor(mod[:, 0:ADA_FIRST, :], PA[:, 1536:1536 + 2 * ADA_FIRST].rearrange("p (a c) -> p a c", c=2),
                              bc(vec[:, 0, V_BADA:V_BADA + ADA_FIRST].unsqueeze(2), [P, ADA_FIRST, 2]), ALU.add)\
               .then_inc(mod_set, 1)
            dve.wait_ge(mod_set, 1)
            dve.tensor_scalar(a1[:, :, :], mod[:, NK:2 * NK, :], 1.0, None, ALU.add).then_inc(a1_set, 1)
            dve.wait_ge(a1_set, 1)
            dve.tensor_tensor(a1[:, :, :], a1[:, :, :], bc(vec[:, 0, V_GMIX:V_GMIX + NK].unsqueeze(2), [P, NK, 2]),
                              ALU.mult).then_inc(a1_set, 1)

            def modulated(src, rs, t, sc_, sh, t_set, hi_set, lo_set):
                def low(k):
                    dve.wait_ge(hi_set, k + 1)
                    for r, cols in enumerate((slice(0, SAMPLE), slice(SAMPLE, TOK))):
                        ins = dve.scalar_tensor_tensor(out=h_lo[:, k, cols], in0=t[:, k % 2, cols], scalar=sh(k, r),
                                                       in1=h_hi[:, k, cols].bitcast(F32), op0=ALU.add, op1=ALU.subtract)
                    ins.then_inc(lo_set, 1)
                for k in range(NK):
                    if k >= 2:
                        dve.wait_ge(lo_set, k - 1)
                    for r, cols in enumerate((slice(0, SAMPLE), slice(SAMPLE, TOK))):
                        ins = dve.scalar_tensor_tensor(out=t[:, k % 2, cols], in0=src[:, k, cols], scalar=sc_[:, k, r:r + 1],
                                                       in1=rs[:, cols], op0=ALU.mult, op1=ALU.mult)
                    ins.then_inc(t_set, 1)
                    if k >= 1:
                        low(k - 1)
                low(NK - 1)

            dve.wait_ge(a1_set, 2)
            dve.wait_ge(rs_done, 1)
            modulated(xT, rstd, h_t, a1, lambda k, r: mod[:, k, r:r + 1], ht_set, hhi_set, hlo_set)
            dve.wait_ge(hlo_set, NK)
            dve.memset(Y[:, :, :, 0:1], 0.0).then_inc(const_set, 1)
            for m in range(4):
                dve.wait_ge(la_abs, m + 1)
                dve.tensor_scalar(by_half(la_m[:, m, :]), halves(PA, m % 2), vec[:, 0, V_BAF + m:V_BAF + m + 1], 0.0,
                                  ALU.add, ALU.min).then_inc(la_min, 1)
            for m in range(4):
                dve.wait_ge(la_ln, m + 1)
                dve.wait_ge(la_min, m + 1)
                dve.tensor_tensor(la_m[:, m, :], la_m[:, m, :], la_e[:, m, :], ALU.subtract).then_inc(la_sub, 1)
                dve.wait_ge(la_sub, m + 1)
                for t in range(NT):
                    ins = dve.tensor_tensor_scan(Y[:, m, t, 1:P + 1], ones[:, :], la_m[:, m, t * P:(t + 1) * P], 0.0,
                                                 ALU.mult, ALU.add)
                ins.then_inc(la_sum, 1)
            dve.wait_ge(tile_freed, 3)
            dve.tensor_scalar(U[:, 0:2, :], U[:, 0:2, :], DK ** -0.5, None, ALU.mult).then_inc(q_scaled, 1)
            dve.wait_ge(q_scaled, 1)
            dve.wait_ge(la_sum, 4)
            dve.wait_ge(const_set, 5)
            dve.wait_ge(tile_freed, 5)
            bank_seq = [0]

            def copied(ins):
                ins.then_inc(lv_cp, 1)
                bank_seq[0] += 1

            def bank():
                return (bank_seq[0] % 4) * BANK

            def args(n):
                b = n % 2
                if n >= 2:
                    dve.wait_ge(lv_ps, 6 * min(n - 1, N_LEVEL))
                yf, yb = y_view(0), y_view(1)
                if n < N_LEVEL:
                    w = 64 >> (n - 1)
                    pairs = P // (2 * w)
                    sh = [P, 2 * NT, pairs, w]

                    def tokens(y, first):
                        return y[:, :, first:first + P].rearrange("p m (a b c) -> p m a b c", b=2, c=w)[:, :, :, 0, :]

                    def border(y):
                        v = y[:, :, w:w + P - w + 1:2 * w] if pairs > 1 else y[:, :, w:w + 1]
                        return v.unsqueeze(3).to_broadcast(sh)

                    q = lvl[:, b, 0:2, :].rearrange("p d (t a b c) -> p (d t) a b c", t=NT, b=2, c=w)
                    k = lvl[:, b, 2:4, :].rearrange("p d (t a b c) -> p (d t) a b c", t=NT, b=2, c=w)

                    def later(y, first):
                        if pairs == 1:
                            return y[:, :, first:first + w].unsqueeze(2)
                        return y[:, :, first - w:first - w + P].rearrange("p m (a b c) -> p m a b c", b=2, c=w)[:, :, :, 1, :]

                    dve.tensor_tensor(q[:, :, :, 1, :], later(yf, w + 1), border(yf), ALU.subtract)
                    dve.tensor_tensor(k[:, :, :, 0, :], border(yf), tokens(yf, 1), ALU.subtract)
                    dve.tensor_tensor(q[:, :, :, 0, :], border(yb), tokens(yb, 0), ALU.subtract)
                    dve.tensor_tensor(k[:, :, :, 1, :], later(yb, w), border(yb), ALU.subtract).then_inc(lv_arg, 1)
                else:
                    q = lvl[:, b, 0:2, :].rearrange("p d (t n) -> p (d t) n", n=P)
                    k = lvl[:, b, 2:4, :].rearrange("p d (t n) -> p (d t) n", n=P)
                    if n == N_LEVEL:
                        dve.tensor_copy(q, yf[:, :, 1:P + 1])
                        dve.tensor_tensor(k, bc(yf[:, :, P:P + 1], [P, 2 * NT, P]), yf[:, :, 1:P + 1], ALU.subtract)\
                           .then_inc(lv_arg, 1)
                    else:
                        dve.tensor_tensor(q, bc(yb[:, :, P:P + 1], [P, 2 * NT, P]), yb[:, :, 0:P], ALU.subtract)
                        dve.tensor_copy(k, yb[:, :, 0:P]).then_inc(lv_arg, 1)

            def decayed(n):
                dve.wait_ge(lv_exp, n)
                dve.tensor_tensor(lvl[:, n % 2, :, :], lvl[:, n % 2, :, :], U[:, 0:4, :], ALU.mult).then_inc(lv_set, 1)

            def score_copy(n):
                for r in range(2):
                    for g, t0 in enumerate((0, 2, 4)):
                        nt = min(2, NT - t0)
                        dve.wait_ge(lv_ps, 6 * n + 3 * r + g + 1)
                        copied(dve.copy_predicated(
                            A[:, r, t0:t0 + nt, :, :].rearrange("p t d n -> p (t d) n"),
                            bc(level_mask[:, n, :].unsqueeze(1), [P, 2 * nt, P]),
                            PA[:, bank():bank() + nt * 256].rearrange("p (m n) -> p m n", n=P)))

            dve.tensor_scalar(lvl[:, 0, 0:2, :], U[:, 0:2, :], 2.0, None, ALU.mult)
            dve.tensor_copy(lvl[:, 0, 2:4, :], U[:, 2:4, :]).then_inc(lv_set, 1)
            for t in range(NT):
                dve.wait_ge(vt_ps, t + 1)
                copied(dve.tensor_copy(v_tok[:, t, :], PA[:, bank():bank() + BANK]))
            dve.wait_ge(mask_in, 32)
            for n in range(1, N_LEVEL + 2):
                args(n)
                if n <= N_LEVEL:
                    score_copy(n - 1)
                decayed(n)
            dve.wait_ge(lv_set, N_LEVEL + 2)
            for d in range(2):
                for g, t0 in enumerate((0, 2, 4)):
                    nt = min(2, NT - t0)
                    dve.wait_ge(kt_ps, 3 * d + g + 1)
                    copied(dve.tensor_copy(kt[:, d, t0:t0 + nt, :].rearrange("p t n -> p (t n)"),
                                           PA[:, bank():bank() + nt * 256]))
            dve.wait_ge(s0_in, 32)
            dve.wait_ge(decay_set, 1)
            for s in range(3):
                for d in range(2):
                    dve.wait_ge(kv_ps, s + 1)
                    cur, nxt = (s, s + 1) if d == 0 else (3 - s, 2 - s)
                    if s:
                        dve.wait_ge(s_set, 4 * s)
                    for dt in range(2):
                        o = s * BANK + d * 256 + dt * P
                        dve.scalar_tensor_tensor(out=S[:, d, nxt, dt, :], in0=S[:, d, cur, dt, :],
                                                 scalar=decay[:, 2 * d + dt, cur:cur + 1], in1=PA[:, o:o + P],
                                                 op0=ALU.mult, op1=ALU.add).then_inc(s_set, 1)
            dve.wait_ge(kv_ps, 4)
            dve.tensor_copy(s_out[:, :, :, :].rearrange("p a b n -> p (a b n)"), PA[:, 3 * BANK:4 * BANK]).then_inc(s_copied, 1)
            for t in range(NT):
                dve.wait_ge(nvt_ps, t + 1)
                dve.tensor_copy(nv_tok[:, t, :], PA[:, (t % 4) * BANK:(t % 4 + 1) * BANK]).then_inc(nvt_cp, 1)
            dve.wait_ge(gr_silu, 1)

            def gla_low(hd):
                dve.wait_ge(og_hid, hd + 1)
                dve.tensor_tensor(og_lo[:, hd, :], oT[:, hd, :], og_hi[:, hd, :].bitcast(F32), ALU.subtract)\
                   .then_inc(og_lod, 1)

            for hd in range(GH):
                dve.wait_ge(og_rsd, hd + 1)
                dve.scalar_tensor_tensor(out=oT[:, hd, :], in0=oT[:, hd, :], scalar=vec[:, 0, V_GGLA:V_GGLA + 1],
                                         in1=og_rs[:, hd % 2, :], op0=ALU.mult, op1=ALU.mult).then_inc(og_n, 1)
                dve.wait_ge(og_n, hd + 1)
                dve.tensor_tensor(oT[:, hd, :], oT[:, hd, :], U[:, 8 + hd, :], ALU.mult).then_inc(og_g, 1)
                dve.wait_ge(sq_rs, hd + 1)
                for x, g in ((0, V_GQ), (1, V_GK)):
                    dve.scalar_tensor_tensor(out=nqk[:, hd + 4 * x, :], in0=nqk[:, hd + 4 * x, :], scalar=vec[:, 0, g:g + 1],
                                             in1=qk_rs[hd][:, x, :], op0=ALU.mult, op1=ALU.mult).then_inc(nqk_set, 1)
                if hd >= 1:
                    gla_low(hd - 1)
            gla_low(GH - 1)

            dve.wait_ge(nqk_set, 8)
            for x in range(2):
                cp = dve.tensor_copy(qk_n[:, x, :], nqk[:, 4 * x, :])
            cp.then_inc(qk_set, 1)
            with dve.Fori(0, 4) as j:
                dve.wait_ge(bias_set, j * 3 + 3)
                for m in range(12):
                    if m == 10:
                        for x in range(2):
                            cp = dve.tensor_copy(qk_n[:, x:x + 1, :], nqk[:, bass.ds((j + 1) % 4 + 4 * x, 1), :])
                        cp.then_inc(qk_set, 1)
                    if m < 10:
                        r, i = m // 5, m % 5
                        dve.wait_ge(sc_ps, j * 10 + (m + 1))
                        if m >= 2:
                            dve.wait_ge(pt_ps, j * 10 + (m - 1))
                        if i < 4:
                            n = KEYS[i][1] * P
                            b0 = KEYS[i][2]
                            dve.tensor_scalar(sc[:, m % 2, n:n + PAST], PA[:, BANK:BANK + PAST], HD ** -0.5, None, ALU.mult,
                                              ALU.max, accum_out=mx[:, 1, m:m + 1])
                            dve.tensor_tensor_reduce(sc[:, m % 2, 0:n], PA[:, 0:n], bias[:, r, b0:b0 + n], HD ** -0.5, -3e38,
                                                     ALU.add, ALU.max, mx[:, 0, m:m + 1]).then_inc(sc_mx, 1)
                            dve.wait_ge(sc_mx, j * 10 + (m + 1))
                            dve.tensor_scalar(nmx[:, m:m + 1], mx[:, 0, m:m + 1], mx[:, 1, m:m + 1], -1.0, ALU.max, ALU.mult)\
                               .then_inc(sc_cp, 1)
                        else:
                            dve.tensor_scalar(sc[:, m % 2, 0:P], PA[:, 0:P], HD ** -0.5, None, ALU.mult,
                                              ALU.max, accum_out=mx[:, 1, m:m + 1]).then_inc(sc_mx, 1)
                            dve.wait_ge(sc_mx, j * 10 + (m + 1))
                            dve.tensor_scalar(nmx[:, m:m + 1], mx[:, 1, m:m + 1], -1.0, None, ALU.mult).then_inc(sc_cp, 1)
                    if m >= 2:
                        q = m - 2
                        r, i = q // 5, q % 5
                        dve.wait_ge(pv_ps, j * 10 + (q + 1))
                        dve.reciprocal(rin[:, q:q + 1], psm[:, q:q + 1]).then_inc(rin_set, 1)
                        dve.wait_ge(rin_set, j * 10 + (q + 1))
                        o = BANK + 256 + 64 * (q % 2)
                        dve.tensor_scalar(o_tok[:, i, bass.ds(j * P + r * HD, HD)], PA[:, o:o + HD], rin[:, q:q + 1], None,
                                          ALU.mult).then_inc(pv_cp, 1)
            for f in range(4):
                dve.wait_ge(on_hi, f + 1)
                ps = PA[:, (f % 2) * 1024:(f % 2) * 1024 + TOK]
                dve.tensor_tensor(ona_lo[:, f, 0:SAMPLE].rearrange("p (r g c) -> p r g c", g=4, c=GC),
                                  ps[:, 0:SAMPLE].rearrange("p (g r c) -> p r g c", g=4, c=GC),
                                  ona_hi[:, f, 0:SAMPLE].bitcast(F32).rearrange("p (r g c) -> p r g c", g=4, c=GC), ALU.subtract)
                dve.tensor_tensor(ona_lo[:, f, SAMPLE:TOK], ps[:, SAMPLE:TOK], ona_hi[:, f, SAMPLE:TOK].bitcast(F32),
                                  ALU.subtract).then_inc(on_lo, 1)
            dve.wait_ge(qk_set, 5)
            with dve.Fori(0, NK) as j:
                for a in range(4):
                    dve.wait_ge(ada2_hid, j * 4 + (a + 1))
                    dve.tensor_tensor(ada_rest_lo[:, a], ada_rest[:, a], ada_rest_hi[:, a % 2].bitcast(F32), ALU.subtract)\
                       .then_inc(ada2_lod, 1)
                dve.wait_ge(mixlo_set, j)
                dve.wait_ge(sg_set, j + 1)
                dve.wait_ge(bg_ps, j + 1)
                dve.tensor_tensor(by_half(t1[:, :]), halves(PJ, 1),
                                  by_half(sg[:, bass.ds(j, 1), :].rearrange("p a n -> p (a n)")), ALU.mult).then_inc(t1_set, 1)
                dve.wait_ge(ada2_used, j * 4 + 4)
                dve.wait_ge(ada2_ps, j)
                dve.tensor_copy(rest_rows[0:4, :], PA[0:4, 1024:1536]).then_inc(ada2_rows, 1)
                dve.wait_ge(bn_ps, j + 1)
                dve.wait_ge(sn_set, j + 1)
                dve.tensor_tensor(by_half(t2[:, :]), halves(PA, 0), by_half(sn[:, :]), ALU.mult).then_inc(t2_set, 1)
                dve.wait_ge(t1_set, j + 1)
                dve.wait_ge(t2_set, j + 1)
                dve.tensor_tensor(t1[:, :], t1[:, :], t2[:, :], ALU.add).then_inc(mixf_set, 1)
                dve.wait_ge(mixhi_set, j + 1)
                dve.tensor_tensor(mix_lo[:, bass.ds(j, 1), :], t1[:, :].unsqueeze(1),
                                  mix_hi[:, bass.ds(j, 1), :].bitcast(F32), ALU.subtract).then_inc(mixlo_set, 1)
                dve.wait_ge(ada2_ps, j + 1)
                dve.tensor_tensor(mod[:, bass.ds(j * 4 + ADA_FIRST, 4), :], PA[:, 1536:1544].rearrange("p (a c) -> p a c", c=2),
                                  bc(vec[:, 0, bass.ds(j * 4 + (V_BADA + ADA_FIRST), 4)].unsqueeze(2), [P, 4, 2]), ALU.add)\
                   .then_inc(ada2_cp, 1)
            dve.wait_ge(mixlo_set, NK)
            dve.memset(zeros[:, :], 0.0).then_inc(zero_set, 1)
            dve.memset(x2_sq[:, 1, :], 0.0).then_inc(zero_set, 1)
            dve.wait_ge(ada2_cp, NK)
            dve.tensor_scalar(a2[:, :, :], mod[:, 4 * NK:5 * NK, :], 1.0, None, ALU.add).then_inc(mod_all, 1)
            dve.wait_ge(mod_all, 1)
            dve.tensor_tensor(a2[:, :, :], a2[:, :, :], bc(vec[:, 0, V_GFFN:V_GFFN + NK].unsqueeze(2), [P, NK, 2]),
                              ALU.mult).then_inc(mod_all, 1)
            dve.wait_ge(mod_all, 2)

            def pieces(pair):
                o = pair * 2 * BANK
                return ((slice(0, HALF), PJ[:, o:o + HALF], 0),
                        (slice(HALF, SAMPLE), PJ[:, o + BANK:o + BANK + SAMPLE - HALF], 0),
                        (slice(SAMPLE, TOK), PJ[:, o + BANK + SAMPLE - HALF:o + BANK + HALF], 1))

            with dve.Fori(0, 4) as i:
                for b in range(2):
                    dve.wait_ge(xc_cp, i * 2 + (b + 1))
                    dve.wait_ge(out_ps, i * 2 + (b + 1))
                    for cols, ps, req in pieces(b):
                        x_ = x2[:, bass.ds(i * 2 + b, 1), cols]
                        ins = dve.scalar_tensor_tensor(
                            out=x_, in0=ps.unsqueeze(1),
                            scalar=mod[:, bass.ds(i * 2 + (2 * NK + b), 1), req:req + 1].rearrange("p a b -> p (a b)"),
                            in1=x_, op0=ALU.mult, op1=ALU.add)
                    ins.then_inc(x2_set, 1)
            dve.wait_ge(rs2_done, 1)
            modulated(x2, rstd2, h2_t, a2, lambda k, r: mod[:, 3 * NK + k, r:r + 1], h2t_set, h2hi_set, h2lo_set)
            dve.wait_ge(h2lo_set, NK)
            dve.memset(ua[:, :], 0.0).then_inc(pad_set, 1)
            dve.memset(ug[:, :], 0.0).then_inc(pad_set, 1)
            n = TOK + 1

            def tap(s, col):
                return vec[:, s, bass.ds(col, 1)]

            with dve.Fori(0, NF) as j:
                dve.wait_ge(actlo_set, j)
                for u, o, first, step, done in ((ua, ca, 0, ca_step, ua_set), (ug, cg, NF, cg_step, ug_set)):
                    dve.wait_ge(done, j + 1)
                    dve.tensor_scalar(o[:, :], u[:, 1:1 + n], tap(1, j + (V_W1 + first)), tap(2, j + first), ALU.mult, ALU.add)\
                       .then_inc(step, 1)
                    dve.wait_ge(step, j * 3 + 1)
                    dve.scalar_tensor_tensor(out=o[:, :], in0=u[:, 0:n], scalar=tap(0, j + (V_W0 + first)), in1=o[:, :],
                                             op0=ALU.mult, op1=ALU.add).then_inc(step, 1)
                    dve.wait_ge(step, j * 3 + 2)
                    dve.scalar_tensor_tensor(out=o[:, :], in0=u[:, 2:2 + n], scalar=tap(1, j + (V_W2 + first)), in1=o[:, :],
                                             op0=ALU.mult, op1=ALU.add).then_inc(step, 1)
                dve.wait_ge(silu_set, j + 1)
                dve.wait_ge(ca_step, j * 3 + 3)
                dve.tensor_tensor(ca[:, :], ca[:, :], cg[:, :], ALU.mult).then_inc(prod_set, 1)
                dve.wait_ge(prod_set, j + 1)
                dve.wait_ge(acthi_set, j + 1)
                jt = bass.ds(j, 1)
                dve.tensor_tensor(act_lo[:, jt, 0:SAMPLE], ca[:, 0:SAMPLE].unsqueeze(1),
                                  act_hi[:, jt, 0:SAMPLE].bitcast(F32), ALU.subtract)
                dve.tensor_tensor(act_lo[:, jt, SAMPLE:TOK], ca[:, SAMPLE + 1:n].unsqueeze(1),
                                  act_hi[:, jt, SAMPLE:TOK].bitcast(F32), ALU.subtract).then_inc(actlo_set, 1)
            with dve.Fori(0, 4) as i:
                for b in range(2):
                    dve.wait_ge(dn_ps, i * 6 + (3 * b + 3))
                    dve.wait_ge(yt_ps, i * 2)
                    for cols, ps, req in pieces(b):
                        ins = dve.scalar_tensor_tensor(
                            out=yT[:, b:b + 1, cols], in0=ps.unsqueeze(1),
                            scalar=mod[:, bass.ds(i * 2 + (5 * NK + b), 1), req:req + 1].rearrange("p a b -> p (a b)"),
                            in1=x2[:, bass.ds(i * 2 + b, 1), cols], op0=ALU.mult, op1=ALU.add)
                    ins.then_inc(y_set, 1)


_INS = ["x_prompt", "x_sample", "c", "cache_na_k", "cache_na_v", "state_gla_fwd", "state_gla_bwd", "c_ctx", "w_ada",
        "b_ada", "g_norm_mix", "w_in", "w_alpha_fwd", "b_alpha_fwd", "w_alpha_bwd", "b_alpha_bwd", "g_gla_norm",
        "g_q_norm", "g_k_norm", "rpb", "w_gla_o", "w_na_o", "w_out", "g_norm_ffn", "w_up", "w_conv", "b_conv", "w_down"]
_OUTS = [(1, CONTEXT, D), (1, SAMPLE, D), (1, 1, CONTEXT, NH, HD), (1, 1, CONTEXT, NH, HD),
         (1, 1, GH, DK, DV), (1, 1, GH, DK, DV)]


def constant_tables():
    import numpy as np

    p = np.arange(P)
    tables = np.zeros((P, 384 + 896 + 2), np.float32)
    tables[:, 0:128] = np.eye(P)
    tables[:, 128:256] = 1
    tables[:, 256:384] = p[:, None] // HD == p[None, :] // HD
    tables[:, 1280:1282] = p[:, None] % 2 == np.arange(2)[None, :]
    col = p % GC
    for at_, first, group, offsets in ((384, 1, None, (-1, 0, 1)), (768, 0, 0, (0, 1)), (1024, 3, 3, (-1, 0))):
        for n, o in enumerate(offsets):
            q = first * GC + col[:, None]
            k = (first + o) * GC + col[None, :]
            start = np.clip(q - WC // 2, 0, GRID_W - WC)
            tables[:, at_ + n * P:at_ + (n + 1) * P] = np.where((k >= start) & (k < start + WC), 0, MASKED)
    masks = np.zeros((P, N_LEVEL, P), np.uint8)
    masks[:, 0, :] = np.eye(P)
    for n in range(1, N_LEVEL):
        w = 64 >> (n - 1)
        b = p // w
        masks[:, n, :] = (b[:, None] // 2 == b[None, :] // 2) & (b[:, None] != b[None, :])
    return tables, masks.view(np.int32)


def kernel(**inputs):
    import numpy as _np
    import concourse.bacc as _bacc
    from concourse import mybir as _mybir
    from concourse.bass_utils import run_bass_kernel_spmd as _run

    nc = _bacc.Bacc("TRN2", target_bir_lowering=False, num_devices=1)
    arrays, args = {}, []

    def add(name, a):
        arrays[f"in_{name}_dram"] = a
        args.append(nc.dram_tensor(f"in_{name}_dram", a.shape, _mybir.dt.from_np(a.dtype), kind="ExternalInput").ap())

    for name in _INS:
        add(name, _np.ascontiguousarray(inputs[name]))
    for name, table in zip(("tables", "level_masks"), constant_tables()):
        add(name, table)
    for i, shape in enumerate(_OUTS):
        args.append(nc.dram_tensor(f"out_{i}_dram", shape, F32, kind="ExternalOutput").ap())
    hybrid_dit_step(nc, *args)
    r = _run(nc, [arrays], core_ids=[0])
    return tuple(r.results[0][f"out_{i}_dram"] for i in range(len(_OUTS)))
```
